# Optimizing a Trainium2 kernel written in Bass

```python
import math
import jax, jax.numpy as jnp
from jax import lax
import numpy as np

D_MODEL = 1024
BATCH = 1
SEQ = 512
DEPTH = 1

CHUNK = 64
Q_BLOCK = 128
MEM_LEN = 256
MIX_WIDTH = D_MODEL
FOX_WIDTH = MIX_WIDTH // 2
FOX_HEAD_DIM = 64
FOX_HEADS = FOX_WIDTH // FOX_HEAD_DIM
GLA_WIDTH = MIX_WIDTH - FOX_WIDTH
GLA_HEADS = 4
GLA_VALUE_DIM = GLA_WIDTH // GLA_HEADS
GLA_KEY_DIM = GLA_VALUE_DIM // 2
GLA_KEY_WIDTH = GLA_HEADS * GLA_KEY_DIM
GLA_GATE_RANK = 16
GLA_TAU = 16.0
XATTN_HEADS = 4
XATTN_HEAD_DIM = D_MODEL // XATTN_HEADS
D_FF = 4 * D_MODEL
EPS = 1e-6
IN_SIZES = (FOX_WIDTH, FOX_WIDTH, FOX_WIDTH, FOX_HEADS,
            GLA_KEY_WIDTH, GLA_KEY_WIDTH, GLA_WIDTH, GLA_GATE_RANK, GLA_WIDTH)
IN_WIDTH = sum(IN_SIZES)


def _split_points():
    return [int(v) for v in np.cumsum(np.array(IN_SIZES))[:-1]]

def rms_norm(x, g):
    xf = x.astype(jnp.float32)
    y = xf * lax.rsqrt(jnp.mean(xf * xf, axis=-1, keepdims=True) + EPS)
    return (y * g.astype(jnp.float32)).astype(x.dtype)

def fox_attention(q, k, v, log_f):
    B, S, H, D = q.shape
    scale = 1.0 / math.sqrt(D)
    c = jnp.transpose(jnp.cumsum(log_f, axis=1), (0, 2, 1))
    outs = []
    for i in range(S // Q_BLOCK):
        start, end = i * Q_BLOCK, (i + 1) * Q_BLOCK
        qb = q[:, start:end]
        kb = k[:, :end]
        vb = v[:, :end]
        s = jnp.einsum('bqhd,bkhd->bhqk', qb, kb).astype(jnp.float32) * scale
        bias = c[:, :, start:end, None] - c[:, :, None, :end]
        q_pos = start + jnp.arange(Q_BLOCK)
        k_pos = jnp.arange(end)
        mask = k_pos[None, :] <= q_pos[:, None]
        s = jnp.where(mask, s + bias, -jnp.inf)
        p = jax.nn.softmax(s, axis=-1)
        outs.append(jnp.einsum('bhqk,bkhd->bqhd', p.astype(vb.dtype), vb))
    return jnp.concatenate(outs, axis=1)

def gla_chunked(q, k, v, g_log):
    B, S, H, Dk = q.shape
    Dv = v.shape[-1]
    N = S // CHUNK

    def to_chunks(a):
        return jnp.transpose(a.astype(jnp.float32).reshape(B, N, CHUNK, H, a.shape[-1]), (0, 3, 1, 2, 4))

    qc = to_chunks(q) * (Dk ** -0.5)
    kc = to_chunks(k)
    vc = to_chunks(v)
    bc = jnp.cumsum(to_chunks(g_log), axis=3)
    q_dec = qc * jnp.exp(bc)
    k_dec = kc * jnp.exp(-bc)
    A = jnp.einsum('bhnck,bhnsk->bhncs', q_dec, k_dec)
    tril = jnp.tril(jnp.ones((CHUNK, CHUNK), dtype=bool))
    A = jnp.where(tril, A, 0.0)
    o_intra = jnp.einsum('bhncs,bhnsv->bhncv', A, vc)
    b_last = bc[:, :, :, -1:, :]
    dS = jnp.einsum('bhnck,bhncv->bhnkv', kc * jnp.exp(b_last - bc), vc)
    decay = jnp.exp(b_last[:, :, :, 0, :])

    def step(state, inp):
        d, ds = inp
        return d[..., None] * state + ds, state

    init = jnp.zeros((B, H, Dk, Dv), jnp.float32)
    _, s_prev = lax.scan(step, init, (jnp.moveaxis(decay, 2, 0), jnp.moveaxis(dS, 2, 0)))
    s_prev = jnp.moveaxis(s_prev, 0, 2)
    o_inter = jnp.einsum('bhnck,bhnkv->bhncv', q_dec, s_prev)
    o = o_intra + o_inter
    o = jnp.transpose(o, (0, 2, 3, 1, 4)).reshape(B, S, H, Dv)
    return o.astype(v.dtype)

def parallel_mixer(xn, w_in, fox_b_f, fox_q_norm_g, fox_k_norm_g,
                   gla_w_gate2, gla_b_gate, gla_out_norm_g, w_out):
    B, S, _ = xn.shape
    proj = xn @ w_in
    fq, fk, fv, ff, gq, gk, gv, glr, gr = jnp.split(proj, _split_points(), axis=-1)
    fq = rms_norm(fq.reshape(B, S, FOX_HEADS, FOX_HEAD_DIM), fox_q_norm_g)
    fk = rms_norm(fk.reshape(B, S, FOX_HEADS, FOX_HEAD_DIM), fox_k_norm_g)
    fv = fv.reshape(B, S, FOX_HEADS, FOX_HEAD_DIM)
    log_f = jax.nn.log_sigmoid((ff + fox_b_f).astype(jnp.float32))
    fox_out = fox_attention(fq, fk, fv, log_f).reshape(B, S, FOX_WIDTH)
    g_log = jax.nn.log_sigmoid((glr @ gla_w_gate2 + gla_b_gate).astype(jnp.float32)) / GLA_TAU
    g_log = g_log.reshape(B, S, GLA_HEADS, GLA_KEY_DIM)
    gla_o = gla_chunked(gq.reshape(B, S, GLA_HEADS, GLA_KEY_DIM),
                        gk.reshape(B, S, GLA_HEADS, GLA_KEY_DIM),
                        gv.reshape(B, S, GLA_HEADS, GLA_VALUE_DIM), g_log)
    gla_o = rms_norm(gla_o, gla_out_norm_g.reshape(GLA_HEADS, GLA_VALUE_DIM)).reshape(B, S, GLA_WIDTH)
    gla_out = gla_o * jax.nn.silu(gr)
    return jnp.concatenate([fox_out, gla_out], axis=-1) @ w_out

def memory_cross_attention(hn, memn, wq, wkv, q_norm_g, k_norm_g, wo):
    B, S, _ = hn.shape
    M = memn.shape[1]
    q = rms_norm((hn @ wq).reshape(B, S, XATTN_HEADS, XATTN_HEAD_DIM), q_norm_g)
    k, v = jnp.split(memn @ wkv, 2, axis=-1)
    k = rms_norm(k.reshape(B, M, XATTN_HEADS, XATTN_HEAD_DIM), k_norm_g)
    v = v.reshape(B, M, XATTN_HEADS, XATTN_HEAD_DIM)
    s = jnp.einsum('bshd,bmhd->bhsm', q, k).astype(jnp.float32) / math.sqrt(XATTN_HEAD_DIM)
    p = jax.nn.softmax(s, axis=-1)
    o = jnp.einsum('bhsm,bmhd->bshd', p.astype(v.dtype), v).reshape(B, S, D_MODEL)
    return o @ wo

def first_inputs(seed: int = 0) -> dict:
    key = jax.random.key(seed)
    ks = jax.random.split(key, 24)
    f32 = jnp.float32

    def nrm(k, shape, scale):
        return jax.random.normal(k, shape, f32) * scale

    def gain(k, shape):
        return jnp.ones(shape, f32) + 0.02 * jax.random.normal(k, shape, f32)

    return {
        "x": nrm(ks[0], (BATCH, SEQ, D_MODEL), 1.0),
        "mem": nrm(ks[1], (BATCH, MEM_LEN, D_MODEL), 1.0),
        "norm_mix_g": gain(ks[2], (D_MODEL,)),
        "w_in": nrm(ks[3], (D_MODEL, IN_WIDTH), D_MODEL ** -0.5),
        "fox_b_f": 2.0 + 0.1 * jax.random.normal(ks[4], (FOX_HEADS,), f32),
        "fox_q_norm_g": gain(ks[5], (FOX_HEAD_DIM,)),
        "fox_k_norm_g": gain(ks[6], (FOX_HEAD_DIM,)),
        "gla_w_gate2": nrm(ks[7], (GLA_GATE_RANK, GLA_KEY_WIDTH), GLA_GATE_RANK ** -0.5),
        "gla_b_gate": nrm(ks[8], (GLA_KEY_WIDTH,), 0.02),
        "gla_out_norm_g": gain(ks[9], (GLA_WIDTH,)),
        "w_out": nrm(ks[10], (MIX_WIDTH, D_MODEL), MIX_WIDTH ** -0.5),
        "norm_xattn_g": gain(ks[11], (D_MODEL,)),
        "norm_mem_g": gain(ks[12], (D_MODEL,)),
        "xattn_wq": nrm(ks[13], (D_MODEL, D_MODEL), D_MODEL ** -0.5),
        "xattn_wkv": nrm(ks[14], (D_MODEL, 2 * D_MODEL), D_MODEL ** -0.5),
        "xattn_q_norm_g": gain(ks[15], (XATTN_HEAD_DIM,)),
        "xattn_k_norm_g": gain(ks[16], (XATTN_HEAD_DIM,)),
        "xattn_wo": nrm(ks[17], (D_MODEL, D_MODEL), D_MODEL ** -0.5),
        "norm_mlp_g": gain(ks[18], (D_MODEL,)),
        "mlp_w1": nrm(ks[19], (D_MODEL, D_FF), D_MODEL ** -0.5),
        "mlp_w2": nrm(ks[20], (D_FF, D_MODEL), D_FF ** -0.5),
    }

def first_block(x, mem, norm_mix_g, w_in, fox_b_f, fox_q_norm_g, fox_k_norm_g,
              gla_w_gate2, gla_b_gate, gla_out_norm_g, w_out,
              norm_xattn_g, norm_mem_g, xattn_wq, xattn_wkv, xattn_q_norm_g,
              xattn_k_norm_g, xattn_wo, norm_mlp_g, mlp_w1, mlp_w2):
    h = x
    for _ in range(DEPTH):
        h = h + parallel_mixer(rms_norm(h, norm_mix_g), w_in, fox_b_f, fox_q_norm_g,
                               fox_k_norm_g, gla_w_gate2, gla_b_gate, gla_out_norm_g, w_out)
        h = h + memory_cross_attention(rms_norm(h, norm_xattn_g), rms_norm(mem, norm_mem_g),
                                       xattn_wq, xattn_wkv, xattn_q_norm_g, xattn_k_norm_g, xattn_wo)
        u = jax.nn.relu(rms_norm(h, norm_mlp_g) @ mlp_w1)
        h = h + (u * u) @ mlp_w2
    return h


DEPTH_2 = 2

N_A_LAYERS = DEPTH_2 // 2
N_B_LAYERS = DEPTH_2 - N_A_LAYERS
CONV_WIDTH = 31
HEAD_DIM = 64
N_HEADS = D_MODEL // HEAD_DIM
N_KV_HEADS = N_HEADS // 4
GROUP = N_HEADS // N_KV_HEADS
WINDOW = 128
BLOCK = 128
N_BUCKETS = 32
MAX_DISTANCE = 128
D_FF_2 = -(-8 * D_MODEL // (3 * 256)) * 256
NEG_INF = -1e30


def rmsnorm(x, g):
    xf = x.astype(jnp.float32)
    xf = xf * lax.rsqrt(jnp.mean(xf * xf, axis=-1, keepdims=True) + EPS)
    return (xf * g.astype(jnp.float32)).astype(x.dtype)

def layernorm(x, g, b):
    xf = x.astype(jnp.float32)
    mu = jnp.mean(xf, axis=-1, keepdims=True)
    var = jnp.mean(jnp.square(xf - mu), axis=-1, keepdims=True)
    y = (xf - mu) * lax.rsqrt(var + EPS) * g.astype(jnp.float32) + b.astype(jnp.float32)
    return y.astype(x.dtype)

def swiglu_ffn(x, w_up, w_down):
    gate, up = jnp.split(x @ w_up, 2, axis=-1)
    return (jax.nn.silu(gate) * up) @ w_down

def conformer_conv(x, w_pw1, b_pw1, w_dw, b_dw, ln_g, ln_b, w_pw2, b_pw2):
    a = jax.nn.glu(x @ w_pw1 + b_pw1, axis=-1)
    y = lax.conv_general_dilated(
        a, w_dw[:, None, :].astype(a.dtype), window_strides=(1,),
        padding=((CONV_WIDTH - 1, 0),),
        dimension_numbers=('NWC', 'WIO', 'NWC'),
        feature_group_count=D_MODEL) + b_dw
    y = jax.nn.silu(layernorm(y, ln_g, ln_b))
    return y @ w_pw2 + b_pw2

def t5_causal_bucket(dist):
    max_exact = N_BUCKETS // 2
    d = jnp.maximum(dist, 0)
    log_ratio = jnp.log(jnp.maximum(d, 1).astype(jnp.float32) / max_exact) / math.log(MAX_DISTANCE / max_exact)
    large = max_exact + (log_ratio * (N_BUCKETS - max_exact)).astype(jnp.int32)
    large = jnp.minimum(large, N_BUCKETS - 1)
    return jnp.where(d < max_exact, d, large)

def banded_sink_attention(q, k, v, sinks, rel_bias):
    B, S = q.shape[0], q.shape[1]
    nb = S // BLOCK
    qb = q.reshape(B, nb, BLOCK, N_KV_HEADS, GROUP, HEAD_DIM)
    kb = k.reshape(B, nb, BLOCK, N_KV_HEADS, HEAD_DIM)
    vb = v.reshape(B, nb, BLOCK, N_KV_HEADS, HEAD_DIM)
    pad = ((0, 0), (1, 0), (0, 0), (0, 0), (0, 0))
    k_band = jnp.concatenate([jnp.pad(kb, pad)[:, :-1], kb], axis=2)
    v_band = jnp.concatenate([jnp.pad(vb, pad)[:, :-1], vb], axis=2)

    s = jnp.einsum('bnqhgd,bnkhd->bnhgqk', qb, k_band,
                   preferred_element_type=jnp.float32) * (HEAD_DIM ** -0.5)

    qi = jnp.arange(BLOCK, dtype=jnp.int32)
    kj = jnp.arange(2 * BLOCK, dtype=jnp.int32)
    dist = qi[:, None] + BLOCK - kj[None, :]
    in_window = (dist >= 0) & (dist < WINDOW)
    bias = rel_bias.astype(jnp.float32)[t5_causal_bucket(dist)]
    bias = jnp.transpose(bias, (2, 0, 1)).reshape(N_KV_HEADS, GROUP, BLOCK, 2 * BLOCK)
    key_pos = (jnp.arange(nb, dtype=jnp.int32)[:, None] - 1) * BLOCK + kj[None, :]
    mask = in_window[None, :, :] & (key_pos >= 0)[:, None, :]

    s = jnp.where(mask[None, :, None, None], s + bias, NEG_INF)
    sink = sinks.astype(jnp.float32).reshape(N_KV_HEADS, GROUP, 1, 1)
    m = jnp.maximum(jnp.max(s, axis=-1, keepdims=True), sink)
    p = jnp.exp(s - m)
    probs = p / (jnp.sum(p, axis=-1, keepdims=True) + jnp.exp(sink - m))
    o = jnp.einsum('bnhgqk,bnkhd->bnqhgd', probs.astype(v.dtype), v_band)
    return o.reshape(B, S, N_HEADS * HEAD_DIM)

def second_inputs(seed: int = 0) -> dict:
    key = jax.random.key(seed)
    ks = jax.random.split(key, 24)
    f32 = jnp.float32
    D, HD, KVD = D_MODEL, N_HEADS * HEAD_DIM, N_KV_HEADS * HEAD_DIM
    nrm = lambda k, shape, scale: jax.random.normal(k, shape, f32) * scale
    gain = lambda k, shape: 1.0 + 0.05 * jax.random.normal(k, shape, f32)
    return {
        "x": jax.random.normal(ks[0], (BATCH, SEQ, D), f32),
        "norm_mix": gain(ks[1], (DEPTH_2, D)),
        "norm_ffn": gain(ks[2], (DEPTH_2, D)),
        "conv_w_pw1": nrm(ks[3], (N_A_LAYERS, D, 2 * D), D ** -0.5),
        "conv_b_pw1": nrm(ks[4], (N_A_LAYERS, 2 * D), 0.02),
        "conv_w_dw": nrm(ks[5], (N_A_LAYERS, CONV_WIDTH, D), CONV_WIDTH ** -0.5),
        "conv_b_dw": nrm(ks[6], (N_A_LAYERS, D), 0.02),
        "conv_ln_g": gain(ks[7], (N_A_LAYERS, D)),
        "conv_ln_b": nrm(ks[8], (N_A_LAYERS, D), 0.02),
        "conv_w_pw2": nrm(ks[9], (N_A_LAYERS, D, D), D ** -0.5),
        "conv_b_pw2": nrm(ks[10], (N_A_LAYERS, D), 0.02),
        "norm_kv": gain(ks[11], (D,)),
        "w_kv": nrm(ks[12], (D, 2 * KVD), D ** -0.5),
        "w_q": nrm(ks[13], (N_B_LAYERS, D, HD), D ** -0.5),
        "w_o": nrm(ks[14], (N_B_LAYERS, HD, D), HD ** -0.5),
        "sinks": nrm(ks[15], (N_B_LAYERS, N_HEADS), 0.5),
        "rel_bias": nrm(ks[16], (N_BUCKETS, N_HEADS), 0.5),
        "ffn_w_up": nrm(ks[17], (DEPTH_2, D, 2 * D_FF_2), D ** -0.5),
        "ffn_w_down": nrm(ks[18], (DEPTH_2, D_FF_2, D), D_FF_2 ** -0.5),
        "norm_final": gain(ks[19], (D,)),
    }

def second_block(x, norm_mix, norm_ffn, conv_w_pw1, conv_b_pw1, conv_w_dw, conv_b_dw,
              conv_ln_g, conv_ln_b, conv_w_pw2, conv_b_pw2, norm_kv, w_kv, w_q, w_o,
              sinks, rel_bias, ffn_w_up, ffn_w_down, norm_final):
    B, S = x.shape[0], x.shape[1]
    h = x
    k_shared = v_shared = None
    for l in range(DEPTH_2):
        if l < N_A_LAYERS:
            i = l
            h = h + conformer_conv(rmsnorm(h, norm_mix[l]), conv_w_pw1[i], conv_b_pw1[i],
                                   conv_w_dw[i], conv_b_dw[i], conv_ln_g[i], conv_ln_b[i],
                                   conv_w_pw2[i], conv_b_pw2[i])
        else:
            if l == N_A_LAYERS:
                kv = rmsnorm(h, norm_kv) @ w_kv
                k_flat, v_flat = jnp.split(kv, 2, axis=-1)
                k_shared = k_flat.reshape(B, S, N_KV_HEADS, HEAD_DIM)
                v_shared = v_flat.reshape(B, S, N_KV_HEADS, HEAD_DIM)
            j = l - N_A_LAYERS
            q = (rmsnorm(h, norm_mix[l]) @ w_q[j]).reshape(B, S, N_HEADS, HEAD_DIM)
            attn = banded_sink_attention(q, k_shared, v_shared, sinks[j], rel_bias)
            h = h + attn @ w_o[j]
        h = h + swiglu_ffn(rmsnorm(h, norm_ffn[l]), ffn_w_up[l], ffn_w_down[l])
    return rmsnorm(h, norm_final)


def setup_inputs(seed=0):
    out = dict(first_inputs(seed))
    for name, value in second_inputs(seed + 1).items():
        if name != "x":
            out[name + "_2"] = value
    return out


def reference(
    x, mem, norm_mix_g, w_in, fox_b_f, fox_q_norm_g, fox_k_norm_g, gla_w_gate2, gla_b_gate,
    gla_out_norm_g, w_out, norm_xattn_g, norm_mem_g, xattn_wq, xattn_wkv, xattn_q_norm_g,
    xattn_k_norm_g, xattn_wo, norm_mlp_g, mlp_w1, mlp_w2, norm_mix_2, norm_ffn_2, conv_w_pw1_2,
    conv_b_pw1_2, conv_w_dw_2, conv_b_dw_2, conv_ln_g_2, conv_ln_b_2, conv_w_pw2_2,
    conv_b_pw2_2, norm_kv_2, w_kv_2, w_q_2, w_o_2, sinks_2, rel_bias_2, ffn_w_up_2,
    ffn_w_down_2, norm_final_2,
):
    x = first_block(
        x, mem, norm_mix_g, w_in, fox_b_f, fox_q_norm_g, fox_k_norm_g, gla_w_gate2, gla_b_gate,
        gla_out_norm_g, w_out, norm_xattn_g, norm_mem_g, xattn_wq, xattn_wkv, xattn_q_norm_g,
        xattn_k_norm_g, xattn_wo, norm_mlp_g, mlp_w1, mlp_w2,
    )
    return second_block(
        x, norm_mix_2, norm_ffn_2, conv_w_pw1_2, conv_b_pw1_2, conv_w_dw_2, conv_b_dw_2,
        conv_ln_g_2, conv_ln_b_2, conv_w_pw2_2, conv_b_pw2_2, norm_kv_2, w_kv_2, w_q_2, w_o_2,
        sinks_2, rel_bias_2, ffn_w_up_2, ffn_w_down_2, norm_final_2,
    )


_drawn_inputs = setup_inputs


def setup_inputs(seed=0):
    import zlib

    import numpy as np

    out = dict(_drawn_inputs(seed))
    spreads = {}
    factors = {'fox_b_f': 2.769,
     'fox_q_norm_g': 8.0,
     'fox_k_norm_g': 8.0,
     'gla_b_gate': 8.0,
     'gla_out_norm_g': 6.251,
     'norm_xattn_g': 8.0,
     'norm_mem_g': 8.0,
     'xattn_q_norm_g': 8.0,
     'xattn_k_norm_g': 8.0,
     'norm_mlp_g': 3.053,
     'conv_b_pw1_2': 49.09,
     'conv_b_dw_2': 27.128,
     'conv_ln_b_2': 53.76,
     'conv_b_pw2_2': 33.712,
     'norm_kv_2': 28.008,
     'sinks_2': 32.184,
     'norm_ffn_2': 8.0,
     'conv_ln_g_2': 8.0,
     'rel_bias_2': 3.026}
    for name, (base, spread) in spreads.items():
        noise = np.random.default_rng([zlib.crc32(name.encode()), seed]).standard_normal(out[name].shape)
        drawn = base * np.exp(spread * noise) if base else spread * noise
        out[name] = __import__('jax').numpy.asarray(drawn.astype(out[name].dtype))
    for name, factor in factors.items():
        out[name] = (out[name] * factor).astype(out[name].dtype)
    return out
```

```python
from contextlib import ExitStack

import numpy as np

import concourse.bass as bass
from concourse import mybir

ALU = mybir.AluOpType
ACT = mybir.ActivationFunctionType
AX = mybir.AxisListType
F32 = mybir.dt.float32
F32R = mybir.dt.float32r

P = 128
SEQ = 512
D = 1024
KC = D // P
TB = SEQ // P
MEM = 256
EPS = 1e-6
NEG = -1e30

FOX_HEADS, FOX_D = 8, 64
FOX_W = FOX_HEADS * FOX_D
GLA_HEADS, GLA_DK, GLA_DV = 4, 64, 128
GLA_KW = GLA_HEADS * GLA_DK
GLA_RANK = 16
GLA_TAU = 16.0
CHUNK = 64
NCH = SEQ // CHUNK
X_HEADS, X_D = 4, 256
FF1 = 4096
FF2 = 2816
CONV = 31
B_HEADS, B_D, B_KV = 16, 64, 4
GROUP = B_HEADS // B_KV
WINDOW = 128
BUCKETS = 32
MAX_DIST = 128

FQ, FK, FV, FF = 0, FOX_W, 2 * FOX_W, 3 * FOX_W
GQ = FF + FOX_HEADS
GK = GQ + GLA_KW
GV = GK + GLA_KW
GLR = GV + GLA_HEADS * GLA_DV
GR = GLR + GLA_RANK

RING = 4
TILE = 8 * P
AHEAD = 2
BANK = 512

STAGES = [("fox_qk", 8, 8), ("fox_v", 4, 4), ("fox_f", 1, 1),
          ("gla_qk", 4, 4), ("gla_v", 4, 4), ("gla_g", 1, 1), ("gla_r", 4, 4),
          ("mix_out", 8, 8),
          ("mem_k", 8, 8), ("mem_v", 8, 4), ("x_q", 8, 8), ("x_out", 8, 8),
          ("mlp_up0", 16, 16), ("mlp_down0", 16, 8), ("mlp_up1", 16, 16), ("mlp_down1", 16, 8),
          ("conv_in", 16, 16), ("conv_out", 8, 8),
          ("ffn_up0", 44, 44), ("ffn_down0", 24, 8),
          ("band_k", 2, 2), ("band_v", 2, 4), ("band_q", 8, 8), ("band_out", 8, 8),
          ("ffn_up1", 44, 44), ("ffn_down1", 24, 8)]


def running(field, start=0):
    out, at = {}, start
    for s in STAGES:
        out[s[0]] = at
        at += s[field]
    out["end"] = at
    return out


TILE0 = running(1)
TILE_N = {s[0]: s[1] for s in STAGES}
OUT_N = {s[0]: s[2] for s in STAGES}
OUT0 = running(2, KC)
for _n in list(OUT0)[[s[0] for s in STAGES].index("mem_k"):]:
    OUT0[_n] += KC
HID0 = {"hidden0": 0, "hidden1": 16, "ffn_hidden0": 32, "ffn_hidden1": 54}

OPERANDS = [("x", 8), ("gla", 4), ("x_q", 8), ("mem", 8), ("mlp", 8), ("hidden0", 16), ("hidden1", 16),
            ("conv", 8), ("conv_ln", 8), ("ffn0", 8), ("ffn_hidden0", 22), ("band_kv", 8), ("band_q", 8),
            ("ffn1", 8), ("ffn_hidden1", 22)]
OP0 = {}
_at = 0
for _n, _c in OPERANDS:
    OP0[_n] = _at
    _at += _c
SUMS = ["x", "x_q", "mem", "mlp", "conv", "ln_mean", "ln_var", "ffn0", "band", "ffn1", "final"]
SS0 = {n: KC * i for i, n in enumerate(SUMS)}
ATT = {"fox": (0, 32, 8), "x": (32, 8, 1), "band": (40, 32, 4)}
ATT_G0 = {"fox": 0, "x": 4, "band": 12}
ATT_AFTER = {"fox": OUT0["gla_qk"], "x": OUT0["x_out"], "band": OUT0["band_out"]}


def group_place(kind, g):
    return (g, 0) if kind == "fox" else (g // 2, 4 * (g % 2))


def band_place(head):
    kv = head // GROUP
    return (kv // 2) * GROUP + head % GROUP, kv % 2


VECS = [("norm_mix_g", 8), ("norm_xattn_g", 8), ("norm_mem_g", 8), ("norm_mlp_g", 8), ("gla_out_norm_g", 4),
        ("fox_q_norm_g", 1), ("fox_k_norm_g", 1), ("xattn_q_norm_g", 2), ("xattn_k_norm_g", 2),
        ("gla_b_gate", 2), ("norm_mix_2", 16), ("norm_ffn_2", 16), ("conv_b_pw1_2", 16), ("conv_b_dw_2", 8),
        ("conv_ln_g_2", 8), ("conv_ln_b_2", 8), ("conv_b_pw2_2", 8), (None, 4),
        ("norm_kv_2", 8), ("norm_final_2", 8), ("conv_w_dw_2", 8 * CONV)]
VCOL = {}
_at = 0
for _n, _c in VECS:
    VCOL[_n] = _at
    _at += _c
NVEC = _at
VROWS = -(-NVEC // P)
VEC_ROWS = [VCOL[None], P, P, NVEC - 3 * P]

CST = {n: i * P for i, n in enumerate(["ident", "ones1024", "head64", "causal", "chunk"])}
NCST = len(CST) * P


def shape_constants():
    c = np.zeros((P, NCST), np.float32)
    i = np.arange(P)
    c[:, CST["ident"]:CST["ident"] + P] = np.eye(P)
    c[:, CST["ones1024"]:CST["ones1024"] + P] = 1.0 / D
    c[:, CST["head64"]:CST["head64"] + P] = (i[:, None] // 64 == i[None] // 64) / 64.0
    c[:, CST["causal"]:CST["causal"] + P] = np.where(i[None] > i[:, None], NEG, 0.0)
    c[:, CST["chunk"]:CST["chunk"] + P] = (i[:, None] <= i[None]) & (i[:, None] // CHUNK == i[None] // CHUNK)
    sel = np.zeros((P, FOX_HEADS, P), np.float32)
    for h in range(FOX_HEADS):
        sel[h, h] = sel[32 + h, h] = 1.0
    dist = 255 - np.arange(3 * P)
    d = np.maximum(dist, 0)
    exact = BUCKETS // 2
    ratio = np.log(np.maximum(d, 1).astype(np.float32) / exact) / np.log(MAX_DIST / exact)
    large = np.minimum(exact + (ratio * (BUCKETS - exact)).astype(np.int32), BUCKETS - 1)
    bucket = np.where(d < exact, d, large)
    inside = (dist >= 0) & (dist < WINDOW)
    hot = ((bucket[None] == np.arange(BUCKETS)[:, None]) & inside[None]).astype(np.float32)
    out = np.broadcast_to(np.where(inside, 0.0, NEG).astype(np.float32), (B_HEADS, 3 * P))
    return c, sel.reshape(P, -1), hot, np.ascontiguousarray(out)


class Steps:

    def __init__(self, engine, sem):
        self.engine, self.sem, self.n, self.i, self.per = engine, sem, 0, None, 0

    def done(self):
        return self.n if self.i is None else self.n + self.i * self.per

    def link(self, ins):
        ins.then_inc(self.sem, 1)
        self.n += 1
        self.engine.wait_ge(self.sem, self.done())

    def enter(self, i, per):
        self.i, self.per, self.at = i, per, self.n

    def leave(self, times):
        assert self.n - self.at == self.per, (self.n - self.at, self.per)
        self.n += self.per * (times - 1)
        self.i = None


def build(nc, A, out):
    with ExitStack() as ctx:
        base = (nc.sbuf_base + 127) // 128 * 128
        at = [base]

        def place(name, shape, dt, offset=None):
            size = -(-4 * int(np.prod(shape[1:])) // 32) * 32
            if offset is None:
                offset, at[0] = at[0], at[0] + size
            return nc.alloc_sbuf_tensor_at(name, shape, dt, offset=offset), offset

        def sem(name):
            return ctx.enter_context(nc.semaphore(name))

        h, _ = place("h", [P, KC, SEQ], F32)
        a_hi, a_at = place("a_hi", [P, KC, SEQ], F32R)
        a_lo, a_lo_at = place("a_lo", [P, KC, SEQ], F32R)
        NH = FF2 // P
        h_hi, hh_at = place("h_hi", [P, NH, SEQ], F32R)
        h_lo, hl_at = place("h_lo", [P, NH, SEQ], F32R)
        w_hi, _ = place("w_hi", [P, RING, TILE], F32R)
        w_lo, _ = place("w_lo", [P, RING, TILE], F32R)
        raw, _ = place("raw", [P, RING, TILE], F32)
        rstd, _ = place("rstd", [P, SEQ], F32)
        ssum, ssum_at = place("ssum", [P, SEQ], F32)
        sq, _ = place("sq", [P, 2, SEQ], F32)
        tmp, tmp_at = place("tmp", [P, 4, SEQ], F32)
        cst, _ = place("cst", [P, NCST], F32)
        ident_r, _ = place("ident_r", [P, P], F32R)
        causal_r, _ = place("causal_r", [P, P], F32R)
        vec, _ = place("vec", [P, VROWS * P], F32)
        eps, _ = place("eps", [P, 1], F32)
        fox_b, _ = place("fox_b", [P, 1], F32)
        rstd_tok, _ = place("rstd_tok", [P, TB], F32)
        neg_max, _ = place("neg_max", [P, 4, 8], F32)
        row_sum, _ = place("row_sum", [P, 4, 8], F32)
        sink_exp, _ = place("sink_exp", [P, 4, 8], F32)
        sinks, _ = place("sinks", [P, B_HEADS], F32)
        decay, _ = place("decay", [P, 2, NCH], F32)
        w_gate, _ = place("w_gate", [GLA_RANK, GLA_KW], F32)
        assert at[0] <= nc.sbuf_top, (at[0], nc.sbuf_top)

        area1, area2, area_end = hh_at + KC * SEQ * 4, hl_at + KC * SEQ * 4, (NH - KC) * SEQ * 4

        def area(start):
            state = [start]

            def take(name, shape, dt=F32):
                t, o = place(name, shape, dt, state[0])
                state[0] = o + 4 * int(np.prod(shape[1:]))
                assert state[0] <= start + area_end, (name, state[0] - start, area_end)
                return t
            return take

        a1, a2 = area(area1), area(area2)
        x_tok = a1("x_tok", [P, TB, D])
        vec_rows = a2("vec_rows", [P, VROWS, P])
        hot = a2("hot", [BUCKETS, 3 * P])
        outside = a2("outside", [B_HEADS, 3 * P])
        rel = a2("rel", [BUCKETS, B_HEADS])
        bias_rows = a2("bias_rows", [B_HEADS, 3 * P])
        a1, a2 = area(area1), area(area2)
        fqk = a1("fqk", [P, 8, SEQ])
        f_p = a1("f_p", [P, 3, BANK])
        f_pt = a1("f_pt", [P, 2, BANK])
        fv = a2("fv", [P, TB, FOX_W])
        sel = a2("sel", [P, FOX_HEADS, P], F32)
        sel_r = a2("sel_r", [P, FOX_HEADS, P], F32R)
        gate_r = a2("gate_r", [P, SEQ], F32R)
        f_o = a2("f_o", [P, 2, BANK])
        a1, a2 = area(area1), area(area2)
        gqk = a1("gqk", [P, 4, SEQ])
        k_dec = a1("k_dec", [P, 2, SEQ])
        k_end = a1("k_end", [P, 2, SEQ])
        k_tok = a1("k_tok", [P, 2, TB, P])
        state = a1("state", [P, 2, NCH, P])
        gv = a2("gv", [P, TB, GLA_HEADS * GLA_DV])
        gr = a2("gr", [P, GLA_HEADS, SEQ])
        g_a = a2("g_a", [P, 2, SEQ])
        g_cum = a2("g_cum", [P, 2, SEQ])
        g_o = a2("g_o", [P, 2, SEQ])
        resets, _ = place("resets", [P, SEQ], F32, ssum_at)
        a1, a2 = area(area1), area(area2)
        xq = a1("xq", [P, KC, SEQ])
        mk = a1("mk", [P, KC, MEM])
        x_o = a1("x_o", [P, 2, BANK])
        m_hi = a2("m_hi", [P, KC, MEM], F32R)
        m_lo = a2("m_lo", [P, KC, MEM], F32R)
        mv = a2("mv", [P, 2, D])
        x_pt = a2("x_pt", [P, 2, BANK])
        mem_tok, _ = place("mem_tok", [P, 2, D], F32, area1)
        x_p, _ = place("x_p", [P, 3, BANK], F32, a_at)
        rstd_mem, _ = place("rstd_mem", [P, MEM], F32, tmp_at + 2 * SEQ * 4)
        PADW = SEQ + CONV - 1
        a1, a2 = area(area1), area(area2)
        glu = a1("glu", [P, KC, PADW])
        conv_y = a2("conv_y", [P, KC, SEQ])
        a1, a2 = area(area1), area(area2)
        bq = a1("bq", [P, KC, SEQ])
        bk = a1("bk", [P, 2, SEQ])
        b_p = a1("b_p", [P, 3, BANK])
        bias = a2("bias", [P, B_HEADS, 2 * P])
        bv = a2("bv", [P, TB, B_KV * B_D])
        b_pt = a2("b_pt", [P, 2, BANK])
        b_o = a2("b_o", [P, 2, BANK])
        a1 = area(area1)
        y_tok = a1("y_tok", [P, TB, D])
        y_feat, _ = place("y_feat", [P, 2, SEQ], F32, a_at)

        bias_dram = nc.dram_tensor("band_bias", (B_HEADS, P, 3 * P), F32, kind="Internal").ap()

        ps = ctx.enter_context(nc.psum_tensor("ps", [P, 8, BANK], F32))
        S_BANK = (4, 5, 6)
        PT_BANK = (7, 3)
        O_BANK = (2, 1)
        OT_BANK = 0

        def c_(name, n=P):
            return cst[:, CST[name]:CST[name] + n]

        ident = c_("ident")

        def v_(name, i=0):
            return vec[:, VCOL[name] + i:VCOL[name] + i + 1]

        consts_in = sem("consts_in")
        sel_in = sem("sel_in")
        x_in = sem("x_in")
        mem_in = sem("mem_in")
        bias_out = sem("bias_out")
        bias_in = sem("bias_in")
        y_out = sem("y_out")
        raw_in = [sem(f"raw_in{i}") for i in range(RING)]
        w_hi_ready = sem("w_hi_ready")
        w_lo_ready = sem("w_lo_ready")
        tile_used = sem("tile_used")
        x_turned = sem("x_turned")
        mem_turned = sem("mem_turned")
        acc_read = sem("acc_read")
        operand_hi = sem("operand_hi")
        operand_lo = sem("operand_lo")
        square_ready = sem("square_ready")
        square_added = sem("square_added")
        stat_ready = sem("stat_ready")
        rstd_ready = sem("rstd_ready")
        head_sq = sem("head_sq")
        head_stat = sem("head_stat")
        head_rstd = sem("head_rstd")
        head_done = sem("head_done")
        consts_ready = sem("consts_ready")
        vec_turned = sem("vec_turned")
        vec_ready = sem("vec_ready")
        bias_hot = sem("bias_hot")
        bias_rows_ready = sem("bias_rows_ready")
        gate_in = sem("gate_in")
        gate_ln = sem("gate_ln")
        gate_ready = sem("gate_ready")
        scores = sem("scores")
        biased = sem("biased")
        max_ready = sem("max_ready")
        probs = sem("probs")
        probs_turned = sem("probs_turned")
        turned_copied = sem("turned_copied")
        pv_done = sem("pv_done")
        sink_in = sem("sink_in")
        sink_ready = sem("sink_ready")
        out_scaled = sem("out_scaled")
        out_turned = sem("out_turned")
        out_hi = sem("out_hi")
        out_lo = sem("out_lo")
        g_z = sem("g_z")
        g_l = sem("g_l")
        g_cum_ready = sem("g_cum_ready")
        g_exp = sem("g_exp")
        g_dec = sem("g_dec")
        k_turned = sem("k_turned")
        k_tok_ready = sem("k_tok_ready")
        ds_ready = sem("ds_ready")
        states_ready = sem("states_ready")
        a_ready = sem("a_ready")
        a_masked = sem("a_masked")
        o_ready = sem("o_ready")
        o_copied = sem("o_copied")
        silu_ready = sem("silu_ready")
        o_done = sem("o_done")
        hidden_sig = sem("hidden_sig")
        hidden_ready = sem("hidden_ready")
        conv_done = sem("conv_done")
        ln_in = sem("ln_in")
        ln_out = sem("ln_out")
        act_step = sem("act_step")
        dve_step = sem("dve_step")
        final_scaled = sem("final_scaled")
        final_turned = sem("final_turned")
        final_copied = sem("final_copied")

        def columns(w, n0, k0=0, kc=KC):
            return w.rearrange("(c p) n -> p c n", p=P)[:, k0:k0 + kc, bass.ds(n0, P)]

        def wide(w, k0, kc, n0, n):
            return w.rearrange("(c p) n -> p c n", p=P)[:, k0:k0 + kc, n0:n0 + n]

        w_in, w_out = A["w_in"], A["w_out"]
        pw1 = A["conv_w_pw1_2"][0]
        pw2 = A["conv_w_pw2_2"][0]
        w_kv = A["w_kv_2"]

        def fixed(tiles):
            return ("fixed", tiles)

        def looped(body, times, source):
            return ("looped", body, times, source)

        def down(w, parts, k_first):
            body = 4 * len(parts) if len(parts) == 3 else 4
            outs = body // len(parts)

            def source(i, j):
                m, part = j // len(parts), j % len(parts)
                k0 = k_first + sum(parts[:part])
                return columns(w, (i * outs + m) * P, k0, parts[part]), parts[part]
            return looped(body, 8 * len(parts) // body, source)

        ffn_parts = (8, 8, 6)
        SOURCES = {
            "fox_qk": looped(4, 2, lambda i, j: (columns(w_in, (4 * i + j) * P), KC)),
            "fox_v": fixed([(wide(w_in, 2 * j, 2, FV, FOX_W), 2) for j in range(4)]),
            "fox_f": fixed([(columns(w_in, FF), KC)]),
            "gla_qk": fixed([(columns(w_in, GQ + j * P), KC) for j in range(4)]),
            "gla_v": fixed([(wide(w_in, 2 * j, 2, GV, GLA_HEADS * GLA_DV), 2) for j in range(4)]),
            "gla_g": fixed([(columns(w_in, GLR), KC)]),
            "gla_r": fixed([(columns(w_in, GR + j * P), KC) for j in range(4)]),
            "mix_out": looped(4, 2, lambda i, j: (columns(w_out, (4 * i + j) * P), KC)),
            "mem_k": looped(4, 2, lambda i, j: (columns(A["xattn_wkv"], (4 * i + j) * P), KC)),
            "mem_v": fixed([(wide(A["xattn_wkv"], 2 * j, 2, D + 512 * half, 512), 2)
                            for half in range(2) for j in range(4)]),
            "x_q": looped(4, 2, lambda i, j: (columns(A["xattn_wq"], (4 * i + j) * P), KC)),
            "x_out": looped(4, 2, lambda i, j: (columns(A["xattn_wo"], (4 * i + j) * P), KC)),
            "mlp_up0": looped(4, 4, lambda i, j: (columns(A["mlp_w1"], (4 * i + j) * P), KC)),
            "mlp_down0": down(A["mlp_w2"], (8, 8), 0),
            "mlp_up1": looped(4, 4, lambda i, j: (columns(A["mlp_w1"], FF1 // 2 + (4 * i + j) * P), KC)),
            "mlp_down1": down(A["mlp_w2"], (8, 8), 16),
            "conv_in": looped(4, 4, lambda i, j: (columns(pw1, (2 * i + j // 2) * P + (j % 2) * D), KC)),
            "conv_out": looped(4, 2, lambda i, j: (columns(pw2, (4 * i + j) * P), KC)),
            "band_k": fixed([(columns(w_kv, j * P), KC) for j in range(2)]),
            "band_v": fixed([(wide(w_kv, 4 * j, 4, B_KV * B_D, B_KV * B_D), 4) for j in range(2)]),
            "band_q": looped(4, 2, lambda i, j: (columns(A["w_q_2"][0], (4 * i + j) * P), KC)),
            "band_out": looped(4, 2, lambda i, j: (columns(A["w_o_2"][0], (4 * i + j) * P), KC)),
        }

        def ffn_up_source(layer):
            return looped(4, 11, lambda i, j: (columns(A["ffn_w_up_2"][layer],
                                                       (2 * i + j // 2) * P + (j % 2) * FF2), KC))

        for layer in range(2):
            SOURCES[f"ffn_up{layer}"] = ffn_up_source(layer)
            SOURCES[f"ffn_down{layer}"] = down(A["ffn_w_down_2"][layer], ffn_parts, 0)

        N_CONST = 1 + 6 + 4 + sum((VCOL[n] + c - 1) // P - VCOL[n] // P + 1 for n, c in VECS
                                  if n and n not in ("fox_q_norm_g", "fox_k_norm_g"))

        block = ctx.enter_context(nc.Block())

        @block.sync
        def _(sp):
            def load_tile(t, i, per, src, kc):
                rounds = t // RING
                if t >= RING:
                    sp.wait_ge(w_lo_ready, t - RING + 1 + per * i)
                n = src.shape[1] * src.shape[2]
                dst = raw[:, t % RING, 0:n].rearrange("p (c n) -> p c n", c=kc)
                sp.dma_start(dst, src).then_inc(raw_in[t % RING], 16)

            def load_stage(name):
                t0 = TILE0[name]
                how = SOURCES[name]
                if how[0] == "fixed":
                    for j, (src, kc) in enumerate(how[1]):
                        load_tile(t0 + j, 0, 0, src, kc)
                    return
                _, body, times, source = how
                start = 0
                if t0 < RING:
                    for j in range(body):
                        load_tile(t0 + j, 0, 0, *source(0, j))
                    start = 1
                if times - start == 1:
                    for j in range(body):
                        load_tile(t0 + body * start + j, 0, 0, *source(start, j))
                    return
                with sp.Fori(start, times) as i:
                    for j in range(body):
                        load_tile(t0 + j, i, body, *source(i, j))

            x_rows = A["x"][0].rearrange("(b p) d -> p b d", p=P)
            sp.dma_start(cst[:], A["shape_cst"]).then_inc(consts_in, 16)
            for b in range(TB):
                sp.dma_start(x_tok[:, b, :], x_rows[:, b, :]).then_inc(x_in, 16)
            n = 1
            for name, rows in VECS:
                if name is None:
                    continue
                v = A[name]
                done = 0
                if name in ("fox_q_norm_g", "fox_k_norm_g"):
                    r = VCOL[name]
                    for half in range(2):
                        sp.dma_start(vec_rows[r:r + 1, 0, half * 64:half * 64 + 64],
                                     v.rearrange("(a d) -> a d", a=1)).then_inc(consts_in, 16)
                        n += 1
                    continue
                flat = {1: "(r p) -> r p", 2: "a (r p) -> (a r) p", 3: "a b (r p) -> (a b r) p"}[len(v.shape)]
                v = v.rearrange(flat, p=P)
                while done < rows:
                    r = VCOL[name] + done
                    m = min(rows - done, P - r % P)
                    sp.dma_start(vec_rows[r % P:r % P + m, r // P, :], v[done:done + m, :]).then_inc(consts_in, 16)
                    n += 1
                    done += m
            sp.dma_start(fox_b[0:FOX_HEADS, :], A["fox_b_f"].rearrange("(h o) -> h o", o=1)).then_inc(consts_in, 16)
            sp.dma_start(w_gate[:], A["gla_w_gate2"]).then_inc(consts_in, 16)
            sp.dma_start(rel[:], A["rel_bias_2"]).then_inc(consts_in, 16)
            sp.dma_start(sinks[:], A["sinks_2"].partition_broadcast(P)).then_inc(consts_in, 16)
            sp.dma_start(hot[:], A["shape_hot"]).then_inc(consts_in, 16)
            sp.dma_start(outside[:], A["shape_outside"]).then_inc(consts_in, 16)
            assert n + 6 == N_CONST, n + 6
            sp.dma_start(sel[:], A["shape_sel"].rearrange("p (h n) -> p h n", h=FOX_HEADS)).then_inc(sel_in, 16)
            load_stage("fox_qk")
            sp.wait_ge(bias_rows_ready, 1)
            sp.dma_start(bias_dram, bias_rows[:].unsqueeze(1).to_broadcast([B_HEADS, P, 3 * P]))\
              .then_inc(bias_out, 16)
            for name in ("fox_v", "fox_f", "gla_qk", "gla_v", "gla_g", "gla_r", "mix_out"):
                load_stage(name)
            sp.wait_ge(operand_lo, OP0["gla"] + 4)
            sp.dma_start(mem_tok[:], A["mem"][0].rearrange("(b p) d -> p b d", p=P)).then_inc(mem_in, 16)
            for name in ("mem_k", "mem_v", "x_q", "x_out", "mlp_up0", "mlp_down0", "mlp_up1", "mlp_down1",
                         "conv_in", "conv_out", "ffn_up0", "ffn_down0", "band_k", "band_v"):
                load_stage(name)
            sp.wait_ge(tile_used, TILE0["band_k"])
            sp.dma_start(bias[:], bass.AP(bias_dram.tensor, P - 1, [[3 * P - 1, P], [3 * P * P, B_HEADS], [1, 2 * P]]))\
              .then_inc(bias_in, 16)
            for name in ("band_q", "band_out", "ffn_up1", "ffn_down1"):
                load_stage(name)
            y_rows = out[0].rearrange("(b p) d -> p b d", p=P)
            sp.wait_ge(final_copied, KC)
            for b in range(TB):
                sp.dma_start(y_rows[:, b, :], y_tok[:, b, :]).then_inc(y_out, 16)
            sp.wait_ge(y_out, 16 * TB)

        @block.tensor
        def _(pe):
            mm = nc.tensor.matmul

            def wait_tile(t, more=0):
                pe.wait_ge(w_lo_ready, t + 1 + more)

            def wait_bank(o, more=0):
                if o >= 4:
                    pe.wait_ge(acc_read, o - 3 + more)

            def three(acc, l_hi, l_lo, r_hi, r_lo, start, stop):
                mm(acc, l_hi, r_hi, start=start, stop=False, skip_group_check=True)
                mm(acc, l_hi, r_lo, start=False, stop=False, skip_group_check=True)
                return mm(acc, l_lo, r_hi, start=False, stop=stop, skip_group_check=True)

            def tile_product(t, o, x_hi, x_lo, k0, kc, first, last, n=SEQ, ready=None):
                slot = t % RING
                acc = ps[:, o % 4, 0:n]
                for k in range(kc):
                    if ready is not None:
                        pe.wait_ge(operand_lo, ready + k + 1)
                    s = slice(k * P, (k + 1) * P)
                    ins = three(acc, w_hi[:, slot, s], w_lo[:, slot, s], x_hi[:, k0 + k, 0:n], x_lo[:, k0 + k, 0:n],
                                first and k == 0, last and k == kc - 1)
                return ins

            def outputs(name, x_hi, x_lo, ready=None, n=SEQ, after_first=None, between=None):
                t0, o0 = TILE0[name], OUT0[name]
                count = OUT_N[name]
                plain = ready is None and after_first is None and between is None and count >= 8
                peel = 0 if plain else 4 if between is None and count >= 12 else count
                for j in range(peel):
                    wait_tile(t0 + j)
                    wait_bank(o0 + j)
                    tile_product(t0 + j, o0 + j, x_hi, x_lo, 0, KC, True, True, n,
                                        ready if j == 0 else None).then_inc(tile_used, 1)
                    if j == 0 and after_first is not None:
                        after_first()
                    if between is not None:
                        between(j)
                if peel < count:
                    with pe.Fori(peel // 4, count // 4) as i:
                        for j in range(4):
                            wait_tile(t0 + j, 4 * i)
                            wait_bank(o0 + j, 4 * i)
                            tile_product(t0 + j, o0 + j, x_hi, x_lo, 0, KC, True, True, n).then_inc(tile_used, 1)

            def down_outputs(name, parts, ready=None):
                t0, o0 = TILE0[name], OUT0[name]
                body = 4 * len(parts)

                def run(i):
                    for m in range(4):
                        k0 = 0
                        for q, kc in enumerate(parts):
                            t = t0 + m * len(parts) + q
                            wait_tile(t, body * i)
                            if q == 0:
                                wait_bank(o0 + m, 4 * i)
                            last = q == len(parts) - 1
                            tile_product(t, o0 + m, h_hi, h_lo, k0, kc, q == 0, last).then_inc(tile_used, 1)
                            k0 += kc
                if ready is not None:
                    pe.wait_ge(operand_lo, ready)
                with pe.Fori(0, 2) as i:
                    run(i)

            def by_token(name, x_hi, x_lo, kc, blocks, n, halves=1):
                t0, o0 = TILE0[name], OUT0[name]
                for half in range(halves):
                    tiles = KC // kc
                    for j in range(tiles):
                        t = t0 + half * tiles + j
                        wait_tile(t)
                        for b in range(blocks):
                            o = o0 + half * blocks + b
                            if j == 0:
                                wait_bank(o)
                            for k in range(kc):
                                c = j * kc + k
                                s = slice(k * n, (k + 1) * n)
                                tb = slice(b * P, (b + 1) * P)
                                w = (w_hi[:, t % RING, s], w_lo[:, t % RING, s])
                                acc = ps[:, o % 4, 0:n]
                                mm(acc, x_hi[:, c, tb], w[0], start=c == 0, stop=False, skip_group_check=True)
                                mm(acc, x_lo[:, c, tb], w[0], start=False, stop=False, skip_group_check=True)
                                ins = mm(acc, x_hi[:, c, tb], w[1], start=False, stop=c == KC - 1,
                                         skip_group_check=True)
                        ins.then_inc(tile_used, 1)

            def stat(name, bank=6, n=SEQ, tokens=0):
                pe.wait_ge(square_added, SS0[name] + KC)
                if tokens:
                    for b in range(tokens):
                        mm(ps[:, 7, b:b + 1], ssum[:, b * P:(b + 1) * P], c_("ones1024", 1), start=True, stop=True)
                mm(ps[:, bank, 0:n], c_("ones1024"), ssum[:, 0:n], start=True, stop=True).then_inc(stat_ready, 1)

            pe.wait_ge(consts_in, 16 * N_CONST)
            pe.wait_ge(x_in, 16 * TB)
            for c in range(KC):
                wait_bank(c)
                for b in range(TB):
                    ins = nc.tensor.transpose(ps[:, c % 4, b * P:(b + 1) * P], x_tok[:, b, c * P:(c + 1) * P], ident)
                ins.then_inc(x_turned, 1)
                if c == 0:
                    for r, n in enumerate(VEC_ROWS):
                        ins = nc.tensor.transpose(ps[:, 4, r * P:r * P + n], vec_rows[0:n, r, :], ident[0:n, 0:n])
                    ins.then_inc(vec_turned, 1)
            mm(ps[0:B_HEADS, 5, 0:3 * P], rel[:], hot[:], start=True, stop=True).then_inc(bias_hot, 1)

            def fox_between(j):
                if j >= 1:
                    norm_stat(j - 1, "head64", [j - 1], SEQ)

            def norm_stat(s, avg, squares, n):
                pe.wait_ge(head_sq, squares[-1] + 1)
                if s >= 2:
                    pe.wait_ge(head_rstd, s - 1)
                for k, w in enumerate(squares):
                    ins = mm(ps[:, 4 + s % 2, 0:n], c_(avg), sq[:, w % 2, 0:n], start=k == 0,
                             stop=k == len(squares) - 1, skip_group_check=True)
                ins.then_inc(head_stat, 1)

            outputs("fox_qk", a_hi, a_lo, ready=OP0["x"], after_first=lambda: stat("x", tokens=TB),
                    between=fox_between)
            norm_stat(7, "head64", [7], SEQ)
            by_token("fox_v", a_hi, a_lo, 2, TB, FOX_W)
            outputs("fox_f", a_hi, a_lo)

            def attention(kind, scores_of, widths, pv_of, o_first):
                u0, units, per = ATT[kind]
                g0 = ATT_G0[kind]
                pe.wait_ge(acc_read, ATT_AFTER[kind])
                probs_at, pt_at, o_at = {"fox": (f_p, f_pt, f_o), "x": (x_p, x_pt, x_o), "band": (b_p, b_pt, b_o)}[kind]
                for s in range(units + 5):
                    if s < units:
                        if u0 + s >= 3:
                            pe.wait_ge(probs, u0 + s - 2)
                        scores_of(s, S_BANK[(u0 + s) % 3]).then_inc(scores, 1)
                    v = s - 2
                    if 0 <= v < units:
                        u = u0 + v
                        pe.wait_ge(probs, u + 1)
                        if u >= 2:
                            pe.wait_ge(turned_copied, u - 1)
                        for b in range(widths(v) // P):
                            ins = nc.tensor.transpose(ps[:, PT_BANK[u % 2], b * P:(b + 1) * P],
                                                      probs_at[:, u % 3, b * P:(b + 1) * P], ident)
                        ins.then_inc(probs_turned, 1)
                    v = s - 3
                    if 0 <= v < units:
                        u = u0 + v
                        g = g0 + v // per
                        pe.wait_ge(turned_copied, u + 1)
                        if v % per == 0 and g >= 2:
                            pe.wait_ge(out_scaled, g - 1)
                        pv_of(v, pt_at[:, u % 2, :], O_BANK[g % 2]).then_inc(pv_done, 1)
                    v = s - 4
                    if v >= 0 and v < units and v % per == per - 1:
                        g = g0 + v // per
                        pe.wait_ge(out_scaled, g + 1)
                        if g >= 1:
                            pe.wait_ge(out_lo, g)
                        for b in range(4):
                            ins = nc.tensor.transpose(ps[:, OT_BANK, b * P:(b + 1) * P],
                                                      o_at[:, g % 2, b * P:(b + 1) * P], ident)
                        ins.then_inc(out_turned, 1)

            def fox_scores(u, bank):
                qb, hd = u // FOX_HEADS, u % FOX_HEADS
                c, p0 = hd // 2, 64 * (hd % 2)
                n = (qb + 1) * P
                if u == 0:
                    pe.wait_ge(head_done, 8)
                    pe.wait_ge(gate_ready, 2)
                mm(ps[:, bank, 0:n], fqk[p0:p0 + 64, c, qb * P:(qb + 1) * P], fqk[p0:p0 + 64, 4 + c, 0:n],
                   start=True, stop=False, skip_group_check=True)
                mm(ps[:, bank, 0:n], sel_r[:, hd, :], gate_r[:, 0:n], start=False, stop=False, skip_group_check=True)
                return mm(ps[:, bank, n - P:n], ident_r[:], causal_r[:], start=False, stop=True, skip_group_check=True)

            def fox_pv(u, pt, bank):
                qb, hd = u // FOX_HEADS, u % FOX_HEADS
                for b in range(qb + 1):
                    ins = mm(ps[:, bank, hd * 64:hd * 64 + 64], pt[:, b * P:(b + 1) * P],
                             fv[:, b, hd * 64:hd * 64 + 64], start=b == 0, stop=b == qb, skip_group_check=True)
                return ins

            attention("fox", fox_scores, lambda u: (u // FOX_HEADS + 1) * P, fox_pv, 0)

            pe.wait_ge(out_lo, 4)
            outputs("gla_qk", a_hi, a_lo)
            by_token("gla_v", a_hi, a_lo, 2, TB, GLA_HEADS * GLA_DV)
            outputs("gla_g", a_hi, a_lo)
            for p in range(2):
                pe.wait_ge(acc_read, OUT0["gla_g"] + 1)
                mm(ps[:, 4 + p, :], w_gate[:, p * P:(p + 1) * P], tmp[0:GLA_RANK, 3, :], start=True, stop=True)\
                    .then_inc(g_z, 1)
            outputs("gla_r", a_hi, a_lo)
            for p in range(2):
                pe.wait_ge(g_dec, 3 * (p + 1))
                for b in range(TB):
                    ins = nc.tensor.transpose(ps[:, 6 + p, b * P:(b + 1) * P], k_end[:, p, b * P:(b + 1) * P], ident)
                ins.then_inc(k_turned, 1)

            def gla_a(hd):
                p, p0 = hd // 2, 64 * (hd % 2)
                bank = 4 + hd % 2
                if hd >= 2:
                    pe.wait_ge(a_masked, hd - 1)
                for b in range(TB):
                    tb = slice(b * P, (b + 1) * P)
                    ins = mm(ps[:, bank, tb], k_dec[p0:p0 + 64, p, tb], gqk[p0:p0 + 64, p, tb], start=True, stop=True)
                ins.then_inc(a_ready, 1)

            gla_a(0)
            gla_a(1)
            pe.wait_ge(acc_read, OUT0["mix_out"])
            for p in range(2):
                pe.wait_ge(k_tok_ready, p + 1)
                for n in range(NCH - 1):
                    b, s0 = n // 2, 64 * (n % 2)
                    for e in range(2):
                        ins = mm(ps[64 * e:64 * e + 64, 2 * p + n % 2, b * P:(b + 1) * P],
                                 k_tok[s0:s0 + 64, p, b, 64 * e:64 * e + 64],
                                 gv[s0:s0 + 64, b, (2 * p + e) * P:(2 * p + e + 1) * P], start=True, stop=True)
                ins.then_inc(ds_ready, 1)
            for hd in range(GLA_HEADS):
                p, p0 = hd // 2, 64 * (hd % 2)
                bank = 6 + hd % 2
                pe.wait_ge(a_masked, hd + 1)
                pe.wait_ge(states_ready, p + 1)
                if hd >= 2:
                    pe.wait_ge(o_copied, hd - 1)
                for b in range(TB):
                    tb = slice(b * P, (b + 1) * P)
                    mm(ps[:, bank, tb], gv[:, b, hd * P:(hd + 1) * P], g_a[:, hd % 2, tb], start=b == 0, stop=False,
                       skip_group_check=True)
                for n in range(1, NCH):
                    ts = slice(n * CHUNK, (n + 1) * CHUNK)
                    ins = mm(ps[:, bank, ts], state[p0:p0 + 64, p, n, :], gqk[p0:p0 + 64, p, ts], start=False,
                             stop=n == NCH - 1, skip_group_check=True)
                ins.then_inc(o_ready, 1)
                if hd + 2 < GLA_HEADS:
                    gla_a(hd + 2)
                pe.wait_ge(head_sq, 8 + hd + 1)
                if hd >= 1:
                    pe.wait_ge(head_rstd, 8 + hd)
                mm(ps[:, 0, :], c_("ones1024"), sq[:, hd % 2, :], start=True, stop=True).then_inc(head_stat, 1)

            pe.wait_ge(out_lo, 4)
            pe.wait_ge(operand_lo, OP0["gla"] + 4)
            pe.wait_ge(head_rstd, 12)
            outputs("mix_out", h_hi, h_lo)

            stat("x_q")
            pe.wait_ge(mem_in, 16)
            for c in range(KC):
                o = OUT0["mem_k"] - KC + c
                wait_bank(o)
                for b in range(2):
                    ins = nc.tensor.transpose(ps[:, o % 4, b * P:(b + 1) * P], mem_tok[:, b, c * P:(c + 1) * P], ident)
                ins.then_inc(mem_turned, 1)

            def mem_between(j):
                if j >= 1 and j % 2 == 0:
                    norm_stat(12 + j // 2 - 1, "ones1024", [12 + j - 2, 12 + j - 1], MEM)

            def mem_stat():
                stat("mem", bank=6, n=MEM, tokens=2)

            outputs("mem_k", m_hi, m_lo, ready=OP0["mem"], n=MEM, after_first=mem_stat, between=mem_between)
            norm_stat(15, "ones1024", [18, 19], MEM)
            by_token("mem_v", m_hi, m_lo, 2, 2, 512, halves=2)

            def xq_between(j):
                if j >= 1 and j % 2 == 0:
                    norm_stat(16 + j // 2 - 1, "ones1024", [20 + j - 2, 20 + j - 1], SEQ)

            outputs("x_q", a_hi, a_lo, ready=OP0["x_q"], between=xq_between)
            norm_stat(19, "ones1024", [26, 27], SEQ)

            def x_scores(u, bank):
                if u == 0:
                    pe.wait_ge(head_done, 20)
                for e in range(2):
                    hd = 2 * (u % 2) + e
                    qb = slice((u // 2) * P, (u // 2 + 1) * P)
                    for k in range(2):
                        ins = mm(ps[:, bank, e * MEM:(e + 1) * MEM], xq[:, 2 * hd + k, qb], mk[:, 2 * hd + k, :],
                                 start=k == 0, stop=k == 1, skip_group_check=True)
                return ins

            def x_pv(u, pt, bank):
                for e in range(2):
                    hd = 2 * (u % 2) + e
                    for b in range(2):
                        ins = mm(ps[:, bank, e * X_D:(e + 1) * X_D], pt[:, (2 * e + b) * P:(2 * e + b + 1) * P],
                                 mv[:, b, hd * X_D:(hd + 1) * X_D], start=b == 0, stop=b == 1, skip_group_check=True)
                return ins

            attention("x", x_scores, lambda u: BANK, x_pv, 4)
            pe.wait_ge(out_lo, 12)
            outputs("x_out", h_hi, h_lo)

            outputs("mlp_up0", a_hi, a_lo, ready=OP0["mlp"], after_first=lambda: stat("mlp"))
            down_outputs("mlp_down0", (8, 8), ready=OP0["hidden0"] + 16)
            outputs("mlp_up1", a_hi, a_lo)
            down_outputs("mlp_down1", (8, 8), ready=OP0["hidden1"] + 16)

            outputs("conv_in", a_hi, a_lo, ready=OP0["conv"], after_first=lambda: stat("conv"))
            stat("ln_mean", bank=4)
            stat("ln_var", bank=5)
            outputs("conv_out", h_hi, h_lo, ready=OP0["conv_ln"])

            def ffn(layer):
                outputs(f"ffn_up{layer}", a_hi, a_lo, ready=OP0[f"ffn{layer}"], after_first=lambda: stat(f"ffn{layer}"))
                down_outputs(f"ffn_down{layer}", ffn_parts, ready=OP0[f"ffn_hidden{layer}"] + NH)

            ffn(0)

            outputs("band_k", a_hi, a_lo, ready=OP0["band_kv"], after_first=lambda: stat("band", tokens=TB))
            by_token("band_v", a_hi, a_lo, 4, TB, B_KV * B_D)
            outputs("band_q", h_hi, h_lo, ready=OP0["band_q"])

            def band_scores(u, bank):
                qb, hp = u // 8, u % 8
                w = P if qb == 0 else 2 * P
                k0 = 0 if qb == 0 else (qb - 1) * P
                for e in range(2):
                    hd = 2 * hp + e
                    kv = hd // GROUP
                    p0 = 64 * (kv % 2)
                    ins = mm(ps[:, bank, e * w:(e + 1) * w], bq_at(hd, p0, qb), bk[p0:p0 + 64, kv // 2, k0:k0 + w],
                             start=True, stop=True)
                return ins

            def bq_at(hd, p0, qb):
                c, half = band_place(hd)
                assert 64 * half == p0
                return bq[p0:p0 + 64, c, qb * P:(qb + 1) * P]

            def band_pv(u, pt, bank):
                qb, hp = u // 8, u % 8
                for e in range(2):
                    hd = 2 * hp + e
                    kv = hd // GROUP
                    blocks = [0] if qb == 0 else [qb - 1, qb]
                    for k, b in enumerate(blocks):
                        s = (e * len(blocks) + k) * P
                        col = (hd % 8) * 64
                        ins = mm(ps[:, bank, col:col + 64], pt[:, s:s + P], bv[:, b, kv * 64:kv * 64 + 64],
                                 start=k == 0, stop=k == len(blocks) - 1, skip_group_check=True)
                return ins

            attention("band", band_scores, lambda u: 2 * P if u < 8 else BANK, band_pv, 12)
            pe.wait_ge(out_lo, 20)
            outputs("band_out", h_hi, h_lo)

            ffn(1)

            stat("final")
            pe.wait_ge(acc_read, OUT0["end"])
            for c in range(KC):
                o = OUT0["end"] + c
                pe.wait_ge(final_scaled, c + 1)
                if c >= 4:
                    pe.wait_ge(final_copied, c - 3)
                for b in range(TB):
                    ins = nc.tensor.transpose(ps[:, o % 4, b * P:(b + 1) * P], y_feat[:, c % 2, b * P:(b + 1) * P], ident)
                ins.then_inc(final_turned, 1)

        @block.scalar
        def _(act):
            me = Steps(act, act_step)

            def split_hi(t, more=0):
                if t >= TILE0["end"]:
                    return
                act.wait_ge(raw_in[t % RING], 16 * (t // RING + 1) + 4 * more)
                if t >= RING:
                    act.wait_ge(tile_used, t - RING + 1 + more)
                nc.scalar.activation(w_hi[:, t % RING, :], raw[:, t % RING, :], ACT.Copy).then_inc(w_hi_ready, 1)

            def ln_exp(out_ap, in_ap, inc, scale=1.0):
                me.link(nc.scalar.activation(out_ap, in_ap, ACT.Ln, bias=eps[:], scale=scale))
                nc.scalar.activation(out_ap, out_ap, ACT.Exp, scale=-0.5).then_inc(inc, 1)

            stats = [0]

            def stat_rstd(n=SEQ, tokens=0, bank=6, to=rstd):
                stats[0] += 1
                act.wait_ge(stat_ready, stats[0])
                if tokens:
                    ln_exp(rstd_tok[:, 0:tokens], ps[:, 7, 0:tokens], rstd_ready)
                ln_exp(to[:, 0:n], ps[:, bank, 0:n], rstd_ready)

            def chunk_hi(op, c, gain, hi, n=SEQ, src=None, o=None):
                act.wait_ge(acc_read, o + 1)
                nc.scalar.activation(hi, src, ACT.Copy, scale=gain).then_inc(operand_hi, 1)

            squares, other_sums = [0], [0]

            def chunk_square(src, n=SEQ):
                k = squares[0]
                if k >= 2:
                    act.wait_ge(square_added, k - 1 + other_sums[0])
                nc.scalar.activation(sq[:, k % 2, 0:n], src, ACT.Square).then_inc(square_ready, 1)
                squares[0] += 1

            def head_square(k, src, n=SEQ):
                nc.scalar.activation(sq[:, k % 2, 0:n], src, ACT.Square).then_inc(head_sq, 1)

            def residual(name, gain, parts=1, hi=a_hi):
                t0, o0 = TILE0[name], OUT0[name]
                for m in range(8):
                    for q in range(parts):
                        split_hi(t0 + m * parts + q + AHEAD)
                    act.wait_ge(acc_read, o0 + m + 1)
                    if gain is not None:
                        nc.scalar.activation(hi[:, m, :], h[:, m, :], ACT.Copy, scale=v_(*gain(m)))\
                            .then_inc(operand_hi, 1)
                    chunk_square(h[:, m, :])

            def splits(name, lo=0, hi=None):
                n = TILE_N[name]
                for j in range(lo, n if hi is None else hi):
                    split_hi(TILE0[name] + j + AHEAD)

            act.wait_ge(consts_in, 16 * N_CONST)
            nc.scalar.activation(ident_r[:], ident, ACT.Copy).then_inc(consts_ready, 1)
            nc.scalar.activation(causal_r[:], c_("causal"), ACT.Copy).then_inc(consts_ready, 1)
            for j in range(AHEAD):
                split_hi(j)
            act.wait_ge(vec_ready, 1)
            for c in range(KC):
                chunk_hi("x", c, v_("norm_mix_g", c), a_hi[:, c, :], src=h[:, c, :], o=c)
                chunk_square(h[:, c, :])

            def head_norms(name, k0, s0, dst, per, n=SEQ):
                t0 = TILE0[name]
                for j in range(8):
                    split_hi(t0 + j + AHEAD)
                    if j == 0 and name == "fox_qk":
                        stat_rstd(tokens=TB)
                    if j == 0 and name == "mem_k":
                        stat_rstd(n=MEM, tokens=2, to=rstd_mem)
                    act.wait_ge(acc_read, OUT0[name] + j + 1)
                    if k0 + j >= 2:
                        act.wait_ge(head_stat, s0 + (j - 2) // per + 1 if j >= 2 else s0)
                    head_square(k0 + j, dst(j), n)
                    if per == 1:
                        if j >= 1:
                            norm(s0 + j - 1, n)
                    elif j >= 3 and j % 2 == 1:
                        norm(s0 + j // 2 - 1, n)
                norm(s0 + 8 // per - 1, n)

            def norm(s, n, bank=None):
                width = GLA_DV if s < 12 else X_D
                act.wait_ge(head_stat, s + 1)
                if s >= 2:
                    act.wait_ge(head_done, s - 1)
                ln_exp(tmp[:, s % 2, 0:n], ps[:, 4 + s % 2 if bank is None else bank, 0:n], head_rstd,
                       1.0 if s < 8 else D / width)

            head_norms("fox_qk", 0, 0, lambda j: fqk[:, j, :], 1)
            splits("fox_v")
            act.wait_ge(sel_in, 16)
            nc.scalar.activation(sel_r[:], sel[:], ACT.Copy).then_inc(gate_ready, 1)
            splits("fox_f")
            act.wait_ge(gate_in, 1)
            rows = slice(0, FOX_HEADS)
            me.link(nc.scalar.activation(tmp[rows, 1, :], tmp[rows, 0, :], ACT.Abs))
            me.link(nc.scalar.activation(tmp[rows, 1, :], tmp[rows, 1, :], ACT.Exp, scale=-1.0))
            nc.scalar.activation(tmp[rows, 1, :], tmp[rows, 1, :], ACT.Ln, bias=1.0).then_inc(gate_ln, 1)

            def attention(kind):
                u0, units, per = ATT[kind]
                g0 = ATT_G0[kind]
                probs_at, pt_at = {"fox": (f_p, f_pt), "x": (x_p, x_pt), "band": (b_p, b_pt)}[kind]
                for s in range(units + 5):
                    if s < units:
                        u = u0 + s
                        g = g0 + s // per
                        if kind == "fox":
                            parts = [(0, (s // 8 + 1) * P, s % 8)]
                        elif kind == "x":
                            parts = [(0, 256, 0), (256, 512, 1)]
                        else:
                            w = P if s < 8 else 2 * P
                            j = 2 * (s % 4)
                            parts = [(0, w, j), (w, 2 * w, j + 1)]
                        act.wait_ge(max_ready, u + 1)
                        if u >= 3 and kind != "band":
                            act.wait_ge(probs_turned, u - 2)
                        if s % per == 0 and g >= 4:
                            act.wait_ge(out_scaled, g - 3)
                        for a, b, j in parts:
                            src = b_p[:, u % 3, a:b] if kind == "band" else ps[:, S_BANK[u % 3], a:b]
                            ins = nc.scalar.activation(probs_at[:, u % 3, a:b], src, ACT.Exp,
                                                       bias=neg_max[:, g % 4, j:j + 1],
                                                       accum_out=row_sum[:, g % 4, j:j + 1])
                        ins.then_inc(probs, 1)
                    v = s - 2
                    if 0 <= v < units and kind == "band":
                        u = u0 + v
                        n = 2 * P if v < 8 else BANK
                        act.wait_ge(probs_turned, u + 1)
                        if u >= 2:
                            act.wait_ge(pv_done, u - 1)
                        nc.scalar.activation(pt_at[:, u % 2, 0:n], ps[:, PT_BANK[u % 2], 0:n], ACT.Copy)\
                            .then_inc(turned_copied, 1)
                    v = s - 3
                    if kind == "band" and 0 <= v < units and v % per == per - 1:
                        g = g0 + v // per
                        act.wait_ge(sink_in, v // per + 1)
                        nc.scalar.activation(sink_exp[:, g % 4, :], sink_exp[:, g % 4, :], ACT.Exp)\
                            .then_inc(sink_ready, 1)
                    v = s - 4
                    if v >= 0 and v < units and v % per == per - 1:
                        g = g0 + v // per
                        qb, c0 = group_place(kind, g - g0)
                        act.wait_ge(out_turned, g + 1)
                        nc.scalar.activation(h_hi[:, c0:c0 + 4, qb * P:(qb + 1) * P],
                                             ps[:, OT_BANK, :].rearrange("p (c q) -> p c q", c=4), ACT.Copy)\
                            .then_inc(out_hi, 1)

            attention("fox")

            splits("gla_qk")
            splits("gla_v")
            splits("gla_g")
            for p in range(2):
                act.wait_ge(g_l, 2 * p + 1)
                me.link(nc.scalar.activation(g_o[:, p, :], g_a[:, p, :], ACT.Abs))
                me.link(nc.scalar.activation(g_o[:, p, :], g_o[:, p, :], ACT.Exp, scale=-1.0))
                nc.scalar.activation(g_o[:, p, :], g_o[:, p, :], ACT.Ln, bias=1.0).then_inc(g_exp, 1)
            for p in range(2):
                act.wait_ge(g_cum_ready, 2 * p + 2)
                nc.scalar.activation(decay[:, p, :], g_cum[:, p, CHUNK - 1:SEQ:CHUNK], ACT.Exp, scale=1.0 / GLA_TAU)
                if p == 1:
                    act.wait_ge(g_dec, 3)
                nc.scalar.activation(tmp[:, 0, :], g_cum[:, p, :], ACT.Exp, scale=1.0 / GLA_TAU).then_inc(g_exp, 1)
                nc.scalar.activation(tmp[:, 1, :], g_cum[:, p, :], ACT.Exp, scale=-1.0 / GLA_TAU).then_inc(g_exp, 1)
                nc.scalar.activation(tmp[:, 2, :], g_a[:, p, :], ACT.Exp, scale=1.0 / GLA_TAU).then_inc(g_exp, 1)
            splits("gla_r")
            for p in range(2):
                act.wait_ge(k_turned, p + 1)
                nc.scalar.activation(k_tok[:, p, :, :].rearrange("p b n -> p (b n)"), ps[:, 6 + p, :], ACT.Copy)\
                    .then_inc(k_tok_ready, 1)
            for hd in range(GLA_HEADS):
                act.wait_ge(acc_read, OUT0["gla_r"] + hd + 1)
                if hd >= 1:
                    act.wait_ge(o_done, hd)
                nc.scalar.activation(tmp[:, 2, :], gr[:, hd, :], ACT.Sigmoid).then_inc(silu_ready, 1)
                act.wait_ge(o_copied, hd + 1)
                if hd >= 2:
                    act.wait_ge(head_stat, 8 + hd - 1)
                head_square(8 + hd, g_o[:, hd % 2, :])
                norm(8 + hd, SEQ, bank=0)
                act.wait_ge(o_done, hd + 1)
                nc.scalar.activation(h_hi[:, 4 + hd, :], tmp[:, 3, :], ACT.Copy).then_inc(operand_hi, 1)

            residual("mix_out", lambda m: ("norm_xattn_g", m))
            stat_rstd()
            for c in range(KC):
                o = OUT0["mem_k"] - KC + c
                act.wait_ge(acc_read, o + 1)
                nc.scalar.activation(m_hi[:, c, :], tmp[:, c % 2, 0:MEM], ACT.Copy, scale=v_("norm_mem_g", c))\
                    .then_inc(operand_hi, 1)
                chunk_square(tmp[:, c % 2, 0:MEM], MEM)
            head_norms("mem_k", 12, 12, lambda j: mk[:, j, :], 2, MEM)
            splits("mem_v")
            head_norms("x_q", 20, 16, lambda j: xq[:, j, :], 2)
            attention("x")
            residual("x_out", lambda m: ("norm_mlp_g", m))

            def relu_squares(name, half):
                t0 = TILE0[name]

                def body(j, i):
                    split_hi(t0 + j + AHEAD, 4 * i)
                    act.wait_ge(hidden_ready, HID0[half] + j + 1 + 4 * i)
                    nc.scalar.activation(h_hi[:, bass.ds(4 * i + j, 1), :].rearrange("p a n -> p (a n)"), tmp[:, 2 + j % 2, :], ACT.Copy).then_inc(operand_hi, 1)
                with act.Fori(0, 4) as i:
                    for j in range(4):
                        body(j, i)

            stat_rstd()
            relu_squares("mlp_up0", "hidden0")
            splits("mlp_down0")
            relu_squares("mlp_up1", "hidden1")
            residual("mlp_down1", lambda m: ("norm_mix_2", m), parts=2)

            stat_rstd()
            for m in range(KC):
                split_hi(TILE0["conv_in"] + 2 * m + AHEAD)
                split_hi(TILE0["conv_in"] + 2 * m + 1 + AHEAD)
                act.wait_ge(acc_read, OUT0["conv_in"] + 2 * m + 2)
                nc.scalar.activation(tmp[:, 2, :], tmp[:, 1, :], ACT.Sigmoid, bias=v_("conv_b_pw1_2", 8 + m))\
                    .then_inc(hidden_sig, 1)
            other_sums[0] = KC
            for c in range(KC):
                act.wait_ge(ln_in, c + 1)
                chunk_square(conv_y[:, c, :])
            stats[0] += 1
            stat_rstd(bank=5)
            for c in range(KC):
                act.wait_ge(ln_in, KC + c + 1)
                if c >= 1:
                    act.wait_ge(ln_out, c)
                nc.scalar.activation(tmp[:, 0, :], conv_y[:, c, :], ACT.Identity, scale=v_("conv_ln_g_2", c),
                                     bias=v_("conv_ln_b_2", c)).then_inc(hidden_sig, 1)
                nc.scalar.activation(tmp[:, 1, :], conv_y[:, c, :], ACT.Sigmoid, scale=v_("conv_ln_g_2", c),
                                     bias=v_("conv_ln_b_2", c)).then_inc(hidden_sig, 1)
                act.wait_ge(ln_out, c + 1)
                nc.scalar.activation(h_hi[:, c, :], tmp[:, 2, :], ACT.Copy).then_inc(operand_hi, 1)
            residual("conv_out", lambda m: ("norm_ffn_2", m))

            def swiglu(layer):
                t0 = TILE0[f"ffn_up{layer}"]
                stat_rstd()
                with act.Fori(0, 11) as i:
                    for m in range(2):
                        split_hi(t0 + 2 * m + AHEAD, 4 * i)
                        split_hi(t0 + 2 * m + 1 + AHEAD, 4 * i)
                        act.wait_ge(acc_read, OUT0[f"ffn_up{layer}"] + 2 * m + 1 + 4 * i)
                        nc.scalar.activation(tmp[:, 1, :], tmp[:, 0, :], ACT.Sigmoid).then_inc(hidden_sig, 1)
                        act.wait_ge(hidden_ready, HID0[f"ffn_hidden{layer}"] + m + 1 + 2 * i)
                        nc.scalar.activation(h_hi[:, bass.ds(2 * i + m, 1), :].rearrange("p a n -> p (a n)"),
                                             tmp[:, 3, :], ACT.Copy).then_inc(operand_hi, 1)

            swiglu(0)
            residual("ffn_down0", lambda m: ("norm_kv_2", m), parts=3)
            splits("band_k", 0, 1)
            stat_rstd(tokens=TB)
            splits("band_k", 1)
            for c in range(KC):
                act.wait_ge(tile_used, TILE0["band_k"])
                nc.scalar.activation(h_hi[:, c, :], h[:, c, :], ACT.Copy, scale=v_("norm_mix_2", 8 + c))\
                    .then_inc(operand_hi, 1)
            splits("band_v")
            splits("band_q")
            attention("band")
            residual("band_out", lambda m: ("norm_ffn_2", 8 + m))
            swiglu(1)
            residual("ffn_down1", None, parts=3)
            stat_rstd()
            for c in range(KC):
                act.wait_ge(final_turned, c + 1)
                nc.scalar.activation(y_tok[:, :, c * P:(c + 1) * P],
                                     ps[:, (OUT0["end"] + c) % 4, :].rearrange("p (b n) -> p b n", b=TB), ACT.Copy)\
                    .then_inc(final_copied, 1)

        @block.vector
        def _(dve):
            me = Steps(dve, dve_step)
            V = nc.vector
            f32 = lambda ap: ap.bitcast(F32)

            def split_lo(t, more=0):
                if t >= TILE0["end"]:
                    return
                dve.wait_ge(w_hi_ready, t + 1 + more)
                V.tensor_tensor(w_lo[:, t % RING, :], raw[:, t % RING, :], f32(w_hi[:, t % RING, :]), ALU.subtract)\
                    .then_inc(w_lo_ready, 1)

            def splits(name, lo=0, hi=None):
                for j in range(lo, TILE_N[name] if hi is None else hi):
                    split_lo(TILE0[name] + j + AHEAD)

            def wait_acc(name, last, more=0):
                dve.wait_ge(tile_used, TILE0[name] + last + 1 + more)

            added = [0]

            def add_square(n=SEQ, fresh=False):
                k = added[0]
                dve.wait_ge(square_ready, added_sq[0] + 1)
                src = sq[:, added_sq[0] % 2, 0:n]
                if fresh:
                    V.tensor_copy(ssum[:, 0:n], src).then_inc(square_added, 1)
                else:
                    dve.wait_ge(square_added, k)
                    V.tensor_tensor(ssum[:, 0:n], ssum[:, 0:n], src, ALU.add).then_inc(square_added, 1)
                added[0] += 1
                added_sq[0] += 1

            added_sq = [0]
            rstds = [0]

            def wait_rstd(n=1):
                rstds[0] += n
                dve.wait_ge(rstd_ready, rstds[0])

            def chunk_lo(lo, hi, src, gain, index):
                dve.wait_ge(operand_hi, index + 1)
                V.scalar_tensor_tensor(lo, src, gain, f32(hi), ALU.mult, ALU.subtract).then_inc(operand_lo, 1)

            def residual(name, op, gain, parts=1, bias_of=None):
                t0, o0 = TILE0[name], OUT0[name]
                for m in range(8):
                    for q in range(parts):
                        split_lo(t0 + m * parts + q + AHEAD)
                    wait_acc(name, m * parts + parts - 1)
                    acc = ps[:, (o0 + m) % 4, :]
                    if bias_of is None:
                        V.tensor_tensor(h[:, m, :], acc, h[:, m, :], ALU.add).then_inc(acc_read, 1)
                    else:
                        V.scalar_tensor_tensor(h[:, m, :], acc, bias_of(m), h[:, m, :], ALU.add, ALU.add)\
                            .then_inc(acc_read, 1)
                    if op is not None:
                        dve.wait_ge(acc_read, o0 + m + 1)
                        chunk_lo(a_lo[:, m, :], a_hi[:, m, :], h[:, m, :], v_(*gain(m)), OP0[op] + m)
                    add_square(fresh=m == 0)

            V.memset(eps[:], EPS).then_inc(consts_ready, 1)
            dve.wait_ge(vec_turned, 1)
            V.tensor_copy(vec[:, P:NVEC], ps[:, 4, P:NVEC])
            me.link(V.tensor_copy(vec[:, 0:VEC_ROWS[0]], ps[:, 4, 0:VEC_ROWS[0]]))
            V.tensor_scalar(v_("fox_q_norm_g"), v_("fox_q_norm_g"), FOX_D ** -0.5, None, ALU.mult)
            V.tensor_scalar(vec[:, VCOL["xattn_q_norm_g"]:VCOL["xattn_q_norm_g"] + 2],
                            vec[:, VCOL["xattn_q_norm_g"]:VCOL["xattn_q_norm_g"] + 2], X_D ** -0.5, None, ALU.mult)\
                .then_inc(vec_ready, 1)
            dve.wait_ge(vec_ready, 1)
            for j in range(AHEAD):
                split_lo(j)
            for c in range(KC):
                dve.wait_ge(x_turned, c + 1)
                V.tensor_copy(h[:, c, :], ps[:, c % 4, :]).then_inc(acc_read, 1)
                dve.wait_ge(acc_read, c + 1)
                chunk_lo(a_lo[:, c, :], a_hi[:, c, :], h[:, c, :], v_("norm_mix_g", c), OP0["x"] + c)
                add_square(fresh=c == 0)
            dve.wait_ge(bias_hot, 1)
            V.tensor_tensor(bias_rows[:], ps[0:B_HEADS, 5, 0:3 * P], outside[:], ALU.add).then_inc(bias_rows_ready, 1)

            def head_norms(name, s0, dst, gain, per, n=SEQ, by=rstd):
                t0, o0 = TILE0[name], OUT0[name]

                def norm(s):
                    dve.wait_ge(head_rstd, s + 1)
                    for k in range(per):
                        j = (s - s0) * per + k
                        ins = V.scalar_tensor_tensor(dst(j), dst(j), gain(j), tmp[:, s % 2, 0:n], ALU.mult, ALU.mult)
                    ins.then_inc(head_done, 1)
                for j in range(8):
                    split_lo(t0 + j + AHEAD)
                    if j == 0 and name == "fox_qk":
                        wait_rstd(2)
                    if j == 0 and name == "mem_k":
                        wait_rstd(2)
                    wait_acc(name, j)
                    V.tensor_tensor(dst(j), ps[:, (o0 + j) % 4, 0:n], by[:, 0:n], ALU.mult).then_inc(acc_read, 1)
                    if per == 1:
                        if j >= 1:
                            norm(s0 + j - 1)
                    elif j >= 3 and j % 2 == 1:
                        norm(s0 + j // 2 - 1)
                norm(s0 + 8 // per - 1)

            head_norms("fox_qk", 0, lambda j: fqk[:, j, :],
                       lambda j: v_("fox_q_norm_g") if j < 4 else v_("fox_k_norm_g"), 1)
            splits("fox_v")

            def values(name, dst, n, blocks, halves=1):
                for half in range(halves):
                    for b in range(blocks):
                        o = OUT0[name] + half * blocks + b
                        wait_acc(name, TILE_N[name] // halves * (half + 1) - 1)
                        V.tensor_scalar(dst(b, half), ps[:, o % 4, 0:n], rstd_tok[:, b:b + 1], None, ALU.mult)\
                            .then_inc(acc_read, 1)

            dve.wait_ge(bias_out, 16)
            values("fox_v", lambda b, half: fv[:, b, :], FOX_W, TB)
            splits("fox_f")
            rows = slice(0, FOX_HEADS)
            o = OUT0["fox_f"]
            wait_acc("fox_f", 0)
            dve.wait_ge(head_done, 8)
            V.tensor_tensor(tmp[rows, 0, :], ps[rows, o % 4, :], rstd[rows, :], ALU.mult).then_inc(acc_read, 1)
            dve.wait_ge(acc_read, o + 1)
            V.tensor_scalar(tmp[rows, 0, :], tmp[rows, 0, :], fox_b[rows, :], None, ALU.add).then_inc(gate_in, 1)
            me.link(V.memset(gate_r[:].bitcast(F32), 0.0))
            me.link(V.memset(tmp[rows, 3, :], 1.0))
            dve.wait_ge(gate_ln, 1)
            me.link(V.scalar_tensor_tensor(tmp[rows, 0, :], tmp[rows, 0, :], 0.0, tmp[rows, 1, :], ALU.min, ALU.subtract))
            me.link(V.tensor_tensor_scan(out=tmp[rows, 2, :], data0=tmp[rows, 3, :], data1=tmp[rows, 0, :],
                                         initial=0.0, op0=ALU.mult, op1=ALU.add))
            me.link(V.tensor_scalar(gate_r[rows, :], tmp[rows, 2, :], -1.0, None, ALU.mult))
            V.scalar_tensor_tensor(gate_r[32:32 + FOX_HEADS, :], tmp[rows, 2, :], -1.0, f32(gate_r[rows, :]),
                                   ALU.mult, ALU.subtract).then_inc(gate_ready, 1)

            def attention(kind):
                u0, units, per = ATT[kind]
                g0 = ATT_G0[kind]
                pt_at, o_at = {"fox": (f_pt, f_o), "x": (x_pt, x_o), "band": (b_pt, b_o)}[kind]
                for s in range(units + 6):
                    if s < units:
                        u = u0 + s
                        g = g0 + s // per
                        dve.wait_ge(scores, u + 1)
                        if s % per == 0 and g >= 4:
                            dve.wait_ge(out_scaled, g - 3)
                        src = ps[:, S_BANK[u % 3], :]
                        if kind == "fox":
                            V.tensor_reduce(neg_max[:, g % 4, s % 8:s % 8 + 1], src[:, 0:(s // 8 + 1) * P], axis=AX.X,
                                            op=ALU.max, negate=True).then_inc(max_ready, 1)
                        elif kind == "x":
                            V.tensor_reduce(neg_max[:, g % 4, 0:2], src.rearrange("p (a n) -> p a n", a=2), axis=AX.X,
                                            op=ALU.max, negate=True).then_inc(max_ready, 1)
                        else:
                            w = P if s < 8 else 2 * P
                            hd = 2 * (s % 8)
                            if s == 0:
                                dve.wait_ge(bias_in, 16)
                            if u >= 3:
                                dve.wait_ge(probs_turned, u - 2)
                            p3 = b_p[:, u % 3, 0:2 * w].rearrange("p (a n) -> p a n", a=2)
                            me.link(V.tensor_tensor(p3, src[:, 0:2 * w].rearrange("p (a n) -> p a n", a=2),
                                                    bias[:, hd:hd + 2, 2 * P - w:2 * P], ALU.add))
                            j = 2 * (s % 4)
                            nm = neg_max[:, g % 4, j:j + 2]
                            me.link(V.tensor_reduce(nm, p3, axis=AX.X, op=ALU.max, negate=True))
                            V.scalar_tensor_tensor(nm, sinks[:, hd:hd + 2], -1.0, nm, ALU.mult, ALU.min)\
                                .then_inc(max_ready, 1)
                    v = s - 2
                    if 0 <= v < units and kind != "band":
                        u = u0 + v
                        n = (v // 8 + 1) * P if kind == "fox" else BANK
                        dve.wait_ge(probs_turned, u + 1)
                        if u >= 2:
                            dve.wait_ge(pv_done, u - 1)
                        V.tensor_copy(pt_at[:, u % 2, 0:n], ps[:, PT_BANK[u % 2], 0:n]).then_inc(turned_copied, 1)
                    v = s - 3
                    if 0 <= v < units and v % per == per - 1:
                        g = g0 + v // per
                        heads = 2 if kind == "x" else 8
                        rs = row_sum[:, g % 4, 0:heads]
                        dve.wait_ge(probs, u0 + v + 1)
                        if kind == "band":
                            hd0 = 8 * ((g - g0) % 2)
                            dve.wait_ge(max_ready, u0 + v + 1)
                            V.tensor_tensor(sink_exp[:, g % 4, :], sinks[:, hd0:hd0 + 8], neg_max[:, g % 4, :], ALU.add)\
                                .then_inc(sink_in, 1)
                            dve.wait_ge(sink_ready, v // per + 1)
                            me.link(V.tensor_tensor(rs, rs, sink_exp[:, g % 4, :], ALU.add))
                        me.link(V.reciprocal(rs, rs))
                        dve.wait_ge(pv_done, u0 + v + 1)
                        if g >= 2:
                            dve.wait_ge(out_turned, g - 1)
                        width = BANK // heads
                        V.tensor_tensor(o_at[:, g % 2, :].rearrange("p (a n) -> p a n", a=heads),
                                        ps[:, O_BANK[g % 2], :].rearrange("p (a n) -> p a n", a=heads),
                                        rs.unsqueeze(2).to_broadcast([P, heads, width]), ALU.mult)\
                            .then_inc(out_scaled, 1)
                    v = s - 5
                    if v >= 0 and v < units and v % per == per - 1:
                        g = g0 + v // per
                        qb, c0 = group_place(kind, g - g0)
                        dve.wait_ge(out_hi, g + 1)
                        V.tensor_tensor(h_lo[:, c0:c0 + 4, qb * P:(qb + 1) * P],
                                        ps[:, OT_BANK, :].rearrange("p (c q) -> p c q", c=4),
                                        f32(h_hi[:, c0:c0 + 4, qb * P:(qb + 1) * P]), ALU.subtract)\
                            .then_inc(out_lo, 1)

            attention("fox")

            t0 = TILE0["gla_qk"]
            for j in range(4):
                split_lo(t0 + j + AHEAD)
                o = OUT0["gla_qk"] + j
                wait_acc("gla_qk", j)
                V.tensor_tensor(gqk[:, j, :], ps[:, o % 4, :], rstd[:], ALU.mult).then_inc(acc_read, 1)
            splits("gla_v")
            values("gla_v", lambda b, half: gv[:, b, :], GLA_HEADS * GLA_DV, TB)
            splits("gla_g")
            o = OUT0["gla_g"]
            wait_acc("gla_g", 0)
            V.tensor_tensor(tmp[0:GLA_RANK, 3, :], ps[0:GLA_RANK, o % 4, :], rstd[0:GLA_RANK, :], ALU.mult)\
                .then_inc(acc_read, 1)
            me.link(V.memset(resets[:], 1.0))
            me.link(V.memset(resets[:, 0:SEQ:CHUNK], 0.0))
            for p in range(2):
                dve.wait_ge(g_z, p + 1)
                V.tensor_scalar(g_a[:, p, :], ps[:, 4 + p, :], v_("gla_b_gate", p), None, ALU.add).then_inc(g_l, 1)
                dve.wait_ge(g_exp, p + 1)
                V.scalar_tensor_tensor(g_a[:, p, :], g_a[:, p, :], 0.0, g_o[:, p, :], ALU.min, ALU.subtract)\
                    .then_inc(g_l, 1)
                dve.wait_ge(g_l, 2 * p + 2)
                V.tensor_tensor_scan(out=g_cum[:, p, :], data0=resets[:], data1=g_a[:, p, :], initial=0.0,
                                     op0=ALU.mult, op1=ALU.add).then_inc(g_cum_ready, 1)
                dve.wait_ge(g_cum_ready, 2 * p + 1)
                cum = g_cum[:, p, :].rearrange("p (n c) -> p n c", c=CHUNK)
                V.tensor_tensor(g_a[:, p, :].rearrange("p (n c) -> p n c", c=CHUNK),
                                cum[:, :, CHUNK - 1:CHUNK].to_broadcast([P, NCH, CHUNK]), cum, ALU.subtract)\
                    .then_inc(g_cum_ready, 1)
            for p in range(2):
                dve.wait_ge(g_exp, 2 + 3 * p + 1)
                V.scalar_tensor_tensor(gqk[:, p, :], gqk[:, p, :], GLA_DK ** -0.5, tmp[:, 0, :], ALU.mult, ALU.mult)\
                    .then_inc(g_dec, 1)
                dve.wait_ge(g_exp, 2 + 3 * p + 2)
                V.tensor_tensor(k_dec[:, p, :], gqk[:, 2 + p, :], tmp[:, 1, :], ALU.mult).then_inc(g_dec, 1)
                dve.wait_ge(g_exp, 2 + 3 * p + 3)
                V.tensor_tensor(k_end[:, p, :], gqk[:, 2 + p, :], tmp[:, 2, :], ALU.mult).then_inc(g_dec, 1)
            t0 = TILE0["gla_r"]
            for j in range(4):
                split_lo(t0 + j + AHEAD)
                o = OUT0["gla_r"] + j
                wait_acc("gla_r", j)
                V.tensor_tensor(gr[:, j, :], ps[:, o % 4, :], rstd[:], ALU.mult).then_inc(acc_read, 1)

            def mask(hd):
                dve.wait_ge(a_ready, hd + 1)
                if hd >= 2:
                    dve.wait_ge(o_ready, hd - 1)
                chunk_mask = c_("chunk").unsqueeze(1).to_broadcast([P, TB, P])
                V.tensor_tensor(g_a[:, hd % 2, :].rearrange("p (b n) -> p b n", b=TB),
                                ps[:, 4 + hd % 2, :].rearrange("p (b n) -> p b n", b=TB), chunk_mask, ALU.mult)\
                    .then_inc(a_masked, 1)

            mask(0)
            mask(1)
            for p in range(2):
                dve.wait_ge(ds_ready, p + 1)
                for n in range(1, NCH):
                    m = n - 1
                    ds = ps[:, 2 * p + m % 2, (m // 2) * P:(m // 2 + 1) * P]
                    if n == 1:
                        ins = V.tensor_copy(state[:, p, n, :], ds)
                    else:
                        ins = V.scalar_tensor_tensor(state[:, p, n, :], state[:, p, m, :], decay[:, p, m:m + 1], ds,
                                                     ALU.mult, ALU.add)
                    if n < NCH - 1:
                        me.link(ins)
                ins.then_inc(states_ready, 1)
            for hd in range(GLA_HEADS):
                dve.wait_ge(o_ready, hd + 1)
                V.tensor_copy(g_o[:, hd % 2, :], ps[:, 6 + hd % 2, :]).then_inc(o_copied, 1)
                if hd + 2 < GLA_HEADS:
                    mask(hd + 2)
                dve.wait_ge(silu_ready, hd + 1)
                me.link(V.tensor_tensor(gr[:, hd, :], gr[:, hd, :], tmp[:, 2, :], ALU.mult))
                dve.wait_ge(head_rstd, 8 + hd + 1)
                V.scalar_tensor_tensor(g_o[:, hd % 2, :], g_o[:, hd % 2, :], v_("gla_out_norm_g", hd),
                                       tmp[:, hd % 2, :], ALU.mult, ALU.mult).then_inc(head_done, 1)
                dve.wait_ge(head_done, 8 + hd + 1)
                V.tensor_tensor(tmp[:, 3, :], g_o[:, hd % 2, :], gr[:, hd, :], ALU.mult).then_inc(o_done, 1)
                dve.wait_ge(operand_hi, OP0["gla"] + hd + 1)
                V.tensor_tensor(h_lo[:, 4 + hd, :], tmp[:, 3, :], f32(h_hi[:, 4 + hd, :]), ALU.subtract)\
                    .then_inc(operand_lo, 1)

            residual("mix_out", "x_q", lambda m: ("norm_xattn_g", m))

            for c in range(KC):
                o = OUT0["mem_k"] - KC + c
                dve.wait_ge(mem_turned, c + 1)
                V.tensor_copy(tmp[:, c % 2, 0:MEM], ps[:, o % 4, 0:MEM]).then_inc(acc_read, 1)
                dve.wait_ge(acc_read, o + 1)
                chunk_lo(m_lo[:, c, :], m_hi[:, c, :], tmp[:, c % 2, 0:MEM], v_("norm_mem_g", c), OP0["mem"] + c)
                if c == 0:
                    dve.wait_ge(stat_ready, 2)
                add_square(n=MEM, fresh=c == 0)
            wait_rstd(1)
            head_norms("mem_k", 12, lambda j: mk[:, j, :], lambda j: v_("xattn_k_norm_g", j % 2), 2, MEM, rstd_mem)
            splits("mem_v")
            values("mem_v", lambda b, half: mv[:, b, 512 * half:512 * half + 512], 512, 2, 2)
            head_norms("x_q", 16, lambda j: xq[:, j, :], lambda j: v_("xattn_q_norm_g", j % 2), 2)
            attention("x")
            residual("x_out", "mlp", lambda m: ("norm_mlp_g", m))

            def relu_squares(name, half):
                t0, o0 = TILE0[name], OUT0[name]
                with dve.Fori(0, 4) as i:
                    for j in range(4):
                        split_lo(t0 + j + AHEAD, 4 * i)
                        wait_acc(name, j, 4 * i)
                        V.tensor_tensor(tmp[:, j % 2, :], ps[:, (o0 + j) % 4, :], rstd[:], ALU.mult)\
                            .then_inc(acc_read, 1)
                        dve.wait_ge(acc_read, o0 + j + 1 + 4 * i)
                        V.scalar_tensor_tensor(tmp[:, 2 + j % 2, :], tmp[:, j % 2, :], 0.0, tmp[:, j % 2, :], ALU.max,
                                               ALU.mult).then_inc(hidden_ready, 1)
                        dve.wait_ge(operand_hi, OP0[half] + j + 1 + 4 * i)
                        V.tensor_tensor(h_lo[:, bass.ds(4 * i + j, 1), :].rearrange("p a n -> p (a n)"),
                                        tmp[:, 2 + j % 2, :],
                                        f32(h_hi[:, bass.ds(4 * i + j, 1), :]).rearrange("p a n -> p (a n)"),
                                        ALU.subtract).then_inc(operand_lo, 1)

            wait_rstd()
            relu_squares("mlp_up0", "hidden0")
            for m in range(8):
                split_lo(TILE0["mlp_down0"] + 2 * m + AHEAD)
                split_lo(TILE0["mlp_down0"] + 2 * m + 1 + AHEAD)
                o = OUT0["mlp_down0"] + m
                wait_acc("mlp_down0", 2 * m + 1)
                V.tensor_tensor(h[:, m, :], ps[:, o % 4, :], h[:, m, :], ALU.add).then_inc(acc_read, 1)
            relu_squares("mlp_up1", "hidden1")
            residual("mlp_down1", "conv", lambda m: ("norm_mix_2", m), parts=2)

            wait_rstd()
            me.link(V.memset(glu[:, :, 0:CONV - 1], 0.0))
            for m in range(KC):
                t0, o0 = TILE0["conv_in"] + 2 * m, OUT0["conv_in"] + 2 * m
                split_lo(t0 + AHEAD)
                wait_acc("conv_in", 2 * m)
                V.tensor_tensor(tmp[:, 0, :], ps[:, o0 % 4, :], rstd[:], ALU.mult).then_inc(acc_read, 1)
                split_lo(t0 + 1 + AHEAD)
                wait_acc("conv_in", 2 * m + 1)
                V.tensor_tensor(tmp[:, 1, :], ps[:, (o0 + 1) % 4, :], rstd[:], ALU.mult).then_inc(acc_read, 1)
                dve.wait_ge(hidden_sig, m + 1)
                me.link(V.scalar_tensor_tensor(glu[:, m, CONV - 1:PADW], tmp[:, 0, :], v_("conv_b_pw1_2", m),
                                               tmp[:, 2, :], ALU.add, ALU.mult))
                y = conv_y[:, m, :]
                wcol = VCOL["conv_w_dw_2"]
                me.link(V.tensor_scalar(y, glu[:, m, 0:SEQ], vec[:, wcol + m:wcol + m + 1], v_("conv_b_dw_2", m),
                                        ALU.mult, ALU.add))
                with dve.Fori(1, CONV) as j:
                    me.enter(j - 1, 1)
                    me.link(V.scalar_tensor_tensor(y, glu[:, m, bass.ds(j, SEQ)],
                                                   vec[:, bass.ds(8 * j + (wcol + m), 1)], y, ALU.mult, ALU.add))
                me.leave(CONV - 1)
                if m == 0:
                    V.tensor_copy(ssum[:], y).then_inc(square_added, 1)
                else:
                    dve.wait_ge(square_added, added[0])
                    V.tensor_tensor(ssum[:], ssum[:], y, ALU.add).then_inc(square_added, 1)
                added[0] += 1
            dve.wait_ge(stat_ready, 6)
            for c in range(KC):
                V.tensor_tensor(conv_y[:, c, :], conv_y[:, c, :], ps[:, 4, :], ALU.subtract).then_inc(ln_in, 1)
                if c >= 1:
                    add_square(fresh=c == 1)
            add_square()
            wait_rstd()
            for c in range(KC):
                V.tensor_tensor(conv_y[:, c, :], conv_y[:, c, :], rstd[:], ALU.mult).then_inc(ln_in, 1)
                dve.wait_ge(hidden_sig, KC + 2 * c + 2)
                V.tensor_tensor(tmp[:, 2, :], tmp[:, 0, :], tmp[:, 1, :], ALU.mult).then_inc(ln_out, 1)
                dve.wait_ge(operand_hi, OP0["conv_ln"] + c + 1)
                V.tensor_tensor(h_lo[:, c, :], tmp[:, 2, :], f32(h_hi[:, c, :]), ALU.subtract).then_inc(operand_lo, 1)
            residual("conv_out", "ffn0", lambda m: ("norm_ffn_2", m), bias_of=lambda m: v_("conv_b_pw2_2", m))

            def swiglu(layer):
                name = f"ffn_up{layer}"
                t0, o0 = TILE0[name], OUT0[name]
                wait_rstd()
                with dve.Fori(0, 11) as i:
                    me.enter(i, 2)
                    for m in range(2):
                        split_lo(t0 + 2 * m + AHEAD, 4 * i)
                        wait_acc(name, 2 * m, 4 * i)
                        V.tensor_tensor(tmp[:, 0, :], ps[:, (o0 + 2 * m) % 4, :], rstd[:], ALU.mult)\
                            .then_inc(acc_read, 1)
                        split_lo(t0 + 2 * m + 1 + AHEAD, 4 * i)
                        wait_acc(name, 2 * m + 1, 4 * i)
                        V.tensor_tensor(tmp[:, 2, :], ps[:, (o0 + 2 * m + 1) % 4, :], rstd[:], ALU.mult)\
                            .then_inc(acc_read, 1)
                        dve.wait_ge(hidden_sig, KC + 16 + 22 * layer + m + 1 + 2 * i)
                        me.link(V.tensor_tensor(tmp[:, 0, :], tmp[:, 0, :], tmp[:, 1, :], ALU.mult))
                        dve.wait_ge(acc_read, o0 + 2 * m + 2 + 4 * i)
                        V.tensor_tensor(tmp[:, 3, :], tmp[:, 0, :], tmp[:, 2, :], ALU.mult).then_inc(hidden_ready, 1)
                        dve.wait_ge(operand_hi, OP0[f"ffn_hidden{layer}"] + m + 1 + 2 * i)
                        V.tensor_tensor(h_lo[:, bass.ds(2 * i + m, 1), :].rearrange("p a n -> p (a n)"),
                                        tmp[:, 3, :],
                                        f32(h_hi[:, bass.ds(2 * i + m, 1), :]).rearrange("p a n -> p (a n)"),
                                        ALU.subtract).then_inc(operand_lo, 1)
                me.leave(11)

            swiglu(0)
            residual("ffn_down0", "band_kv", lambda m: ("norm_kv_2", m), parts=3)
            splits("band_k", 0, 1)
            wait_rstd(2)

            def band_key(j):
                o = OUT0["band_k"] + j
                wait_acc("band_k", j)
                V.tensor_tensor(bk[:, j, :], ps[:, o % 4, :], rstd[:], ALU.mult).then_inc(acc_read, 1)

            band_key(0)
            splits("band_k", 1)
            band_key(1)
            for c in range(KC):
                chunk_lo(h_lo[:, c, :], h_hi[:, c, :], h[:, c, :], v_("norm_mix_2", 8 + c), OP0["band_q"] + c)
            splits("band_v")
            values("band_v", lambda b, half: bv[:, b, :], B_KV * B_D, TB)
            for j in range(8):
                split_lo(TILE0["band_q"] + j + AHEAD)
                o = OUT0["band_q"] + j
                wait_acc("band_q", j)
                for half in range(2):
                    hd = 2 * j + half
                    c, dst_half = band_place(hd)
                    ins = V.scalar_tensor_tensor(bq[64 * dst_half:64 * dst_half + 64, c, :],
                                                 ps[64 * half:64 * half + 64, o % 4, :], B_D ** -0.5,
                                                 rstd[64 * half:64 * half + 64, :], ALU.mult, ALU.mult)
                ins.then_inc(acc_read, 1)
            attention("band")
            residual("band_out", "ffn1", lambda m: ("norm_ffn_2", 8 + m))
            swiglu(1)
            residual("ffn_down1", None, None, parts=3)
            wait_rstd()
            for c in range(KC):
                if c >= 2:
                    dve.wait_ge(final_turned, c - 1)
                V.scalar_tensor_tensor(y_feat[:, c % 2, :], h[:, c, :], v_("norm_final_2", c), rstd[:], ALU.mult,
                                       ALU.mult).then_inc(final_scaled, 1)


def kernel(**inputs):
    import concourse.bacc as bacc
    from concourse.bass_utils import run_bass_kernel_spmd

    nc = bacc.Bacc("TRN2", target_bir_lowering=False, num_devices=1)
    cst, sel, hot, outside = shape_constants()
    arrays = {name: np.ascontiguousarray(a) for name, a in inputs.items()}
    arrays.update(shape_cst=cst, shape_sel=sel, shape_hot=hot, shape_outside=outside)
    A = {name: nc.dram_tensor(f"in_{name}", a.shape, mybir.dt.from_np(a.dtype), kind="ExternalInput").ap()
         for name, a in arrays.items()}
    out = nc.dram_tensor("out", (1, SEQ, D), F32, kind="ExternalOutput").ap()
    build(nc, A, out)
    r = run_bass_kernel_spmd(nc, [{f"in_{name}": a for name, a in arrays.items()}], core_ids=[0])
    return r.results[0]["out"]
```

```python
from contextlib import ExitStack

import numpy as np

import concourse.bass as bass
from concourse import mybir

ALU = mybir.AluOpType
ACT = mybir.ActivationFunctionType
AX = mybir.AxisListType
F32 = mybir.dt.float32
F32R = mybir.dt.float32r

P = 128
SEQ = 512
D = 1024
KC = D // P
TB = SEQ // P
MEM = 256
EPS = 1e-6
NEG = -1e30

FOX_HEADS, FOX_D = 8, 64
FOX_W = FOX_HEADS * FOX_D
GLA_HEADS, GLA_DK, GLA_DV = 4, 64, 128
GLA_KW = GLA_HEADS * GLA_DK
GLA_RANK = 16
GLA_TAU = 16.0
CHUNK = 64
NCH = SEQ // CHUNK
X_HEADS, X_D = 4, 256
FF1 = 4096
FF2 = 2816
CONV = 31
B_HEADS, B_D, B_KV = 16, 64, 4
GROUP = B_HEADS // B_KV
WINDOW = 128
BUCKETS = 32
MAX_DIST = 128

FQ, FK, FV, FF = 0, FOX_W, 2 * FOX_W, 3 * FOX_W
GQ = FF + FOX_HEADS
GK = GQ + GLA_KW
GV = GK + GLA_KW
GLR = GV + GLA_HEADS * GLA_DV
GR = GLR + GLA_RANK

RING = 4
TILE = 8 * P
AHEAD = 2
BANK = 512

STAGES = [("fox_qk", 8, 8), ("fox_f", 1, 1), ("fox_v", 4, 4),
          ("gla_qk", 4, 4), ("gla_v", 4, 4), ("gla_g", 1, 1), ("gla_r", 4, 4),
          ("mix_out", 8, 8),
          ("mem_k", 8, 8), ("mem_v", 8, 4), ("x_q", 8, 8), ("x_out", 8, 8),
          ("mlp_up0", 16, 16), ("mlp_down0", 16, 8), ("mlp_up1", 16, 16), ("mlp_down1", 16, 8),
          ("conv_in", 16, 16), ("conv_out", 8, 8),
          ("ffn_up0", 44, 44), ("ffn_down0", 24, 8),
          ("band_q0", 2, 2), ("band_k", 2, 2), ("band_v", 2, 4), ("band_q1", 6, 6), ("band_out", 8, 8),
          ("ffn_up1", 44, 44), ("ffn_down1", 24, 8)]


def running(field, start=0):
    out, at = {}, start
    for s in STAGES:
        out[s[0]] = at
        at += s[field]
    out["end"] = at
    return out


TILE0 = running(1)
TILE_N = {s[0]: s[1] for s in STAGES}
OUT_N = {s[0]: s[2] for s in STAGES}
OUT0 = running(2, KC)
for _n in list(OUT0)[[s[0] for s in STAGES].index("mem_k"):]:
    OUT0[_n] += KC
HID0 = {"hidden0": 0, "hidden1": 16, "ffn_hidden0": 32, "ffn_hidden1": 54}

OPERANDS = [("x", 8), ("gla", 4), ("x_q", 8), ("mem", 8), ("mlp", 8), ("hidden0", 16), ("hidden1", 16),
            ("conv", 8), ("conv_ln", 8), ("ffn0", 8), ("ffn_hidden0", 22), ("band_q", 8), ("band_kv", 8),
            ("ffn1", 8), ("ffn_hidden1", 22)]
OP0 = {}
_at = 0
for _n, _c in OPERANDS:
    OP0[_n] = _at
    _at += _c
SUMS = ["x", "x_q", "mem", "mlp", "conv", "ln_mean", "ln_var", "ffn0", "band", "ffn1", "final"]
SS0 = {n: KC * i for i, n in enumerate(SUMS)}
ATT = {"fox": (0, 32, 8), "x": (32, 8, 1), "band": (40, 32, 4)}
ATT_G0 = {"fox": 0, "x": 4, "band": 12}
PV_STEP = {"fox": 3, "x": 3, "band": 4}
ATT_AFTER = {"fox": OUT0["gla_qk"], "x": OUT0["x_out"], "band": OUT0["band_q1"]}


PE_CONV = (1, 3, 5, 7)
DIAG_HALF = 16


def group_place(kind, g, operand):
    if kind == "band":
        return operand[:, g, :]
    qb, c0 = (g, 0) if kind == "fox" else (g // 2, 4 * (g % 2))
    return operand[:, c0:c0 + 4, qb * P:(qb + 1) * P]


def band_width(unit):
    return 2 * P if unit % TB == 0 else 4 * P


def beside(kind, unit):
    stage, first = {"fox": ("gla_qk", 0), "x": (None, 0), "band": ("band_q1", 2)}[kind]
    at = unit - first
    return (stage, at // 4, at % 4) if stage and 0 <= at < 4 * TILE_N[stage] else None


EARLY_OUT, EARLY_CHUNKS = 1, 6
EARLY_UNIT = ATT["band"][1] - EARLY_CHUNKS


def band_place(head):
    kv = head // GROUP
    return (kv // 2) * GROUP + head % GROUP, kv % 2


VECS = [("norm_mix_g", 8), ("norm_xattn_g", 8), ("norm_mem_g", 8), ("norm_mlp_g", 8), ("gla_out_norm_g", 4),
        ("fox_q_norm_g", 1), ("fox_k_norm_g", 1), ("xattn_q_norm_g", 2), ("xattn_k_norm_g", 2),
        ("gla_b_gate", 2), ("norm_mix_2", 16), ("norm_ffn_2", 16), ("conv_b_pw1_2", 16), ("conv_b_dw_2", 8),
        ("conv_ln_g_2", 8), ("conv_ln_b_2", 8), ("conv_b_pw2_2", 8), (None, 4),
        ("norm_kv_2", 8), ("norm_final_2", 8), ("conv_w_dw_2", 8 * CONV)]
VCOL = {}
_at = 0
for _n, _c in VECS:
    VCOL[_n] = _at
    _at += _c
NVEC = _at
VROWS = -(-NVEC // P)
VEC_ROWS = [VCOL[None], P, P, NVEC - 3 * P]

CST = {n: i * P for i, n in enumerate(["ident", "ones1024", "head64", "causal", "chunk"])}
NCST = len(CST) * P


def shape_constants():
    c = np.zeros((P, NCST), np.float32)
    i = np.arange(P)
    c[:, CST["ident"]:CST["ident"] + P] = np.eye(P)
    c[:, CST["ones1024"]:CST["ones1024"] + P] = 1.0 / D
    c[:, CST["head64"]:CST["head64"] + P] = (i[:, None] // 64 == i[None] // 64) / 64.0
    c[:, CST["causal"]:CST["causal"] + P] = np.where(i[None] > i[:, None], NEG, 0.0)
    c[:, CST["chunk"]:CST["chunk"] + P] = (i[:, None] <= i[None]) & (i[:, None] // CHUNK == i[None] // CHUNK)
    sel = np.zeros((P, FOX_HEADS, P), np.float32)
    for h in range(FOX_HEADS):
        sel[h, h] = sel[32 + h, h] = 1.0
    dist = 255 - np.arange(3 * P)
    d = np.maximum(dist, 0)
    exact = BUCKETS // 2
    ratio = np.log(np.maximum(d, 1).astype(np.float32) / exact) / np.log(MAX_DIST / exact)
    large = np.minimum(exact + (ratio * (BUCKETS - exact)).astype(np.int32), BUCKETS - 1)
    bucket = np.where(d < exact, d, large)
    inside = (dist >= 0) & (dist < WINDOW)
    hot = ((bucket[None] == np.arange(BUCKETS)[:, None]) & inside[None]).astype(np.float32)
    out = np.broadcast_to(np.where(inside, 0.0, NEG).astype(np.float32), (B_HEADS, 3 * P))
    return c, sel.reshape(P, -1), hot, np.ascontiguousarray(out)


class Steps:

    def __init__(self, engine, sem):
        self.engine, self.sem, self.n, self.i, self.per = engine, sem, 0, None, 0

    def done(self):
        return self.n if self.i is None else self.n + self.i * self.per

    def link(self, ins):
        ins.then_inc(self.sem, 1)
        self.n += 1
        self.engine.wait_ge(self.sem, self.done())

    def enter(self, i, per):
        self.i, self.per, self.at = i, per, self.n

    def leave(self, times):
        assert self.n - self.at == self.per, (self.n - self.at, self.per)
        self.n += self.per * (times - 1)
        self.i = None


def build(nc, A, out):
    with ExitStack() as ctx:
        base = (nc.sbuf_base + 127) // 128 * 128
        at = [base]

        def place(name, shape, dt, offset=None):
            size = -(-4 * int(np.prod(shape[1:])) // 32) * 32
            if offset is None:
                offset, at[0] = at[0], at[0] + size
            return nc.alloc_sbuf_tensor_at(name, shape, dt, offset=offset), offset

        def sem(name):
            return ctx.enter_context(nc.semaphore(name))

        h, _ = place("h", [P, KC, SEQ], F32)
        a_hi, a_at = place("a_hi", [P, KC, SEQ], F32R)
        a_lo, a_lo_at = place("a_lo", [P, KC, SEQ], F32R)
        NH = FF2 // P
        h_hi, hh_at = place("h_hi", [P, NH, SEQ], F32R)
        h_lo, hl_at = place("h_lo", [P, NH, SEQ], F32R)
        w_hi, _ = place("w_hi", [P, RING, TILE], F32R)
        w_lo, _ = place("w_lo", [P, RING, TILE], F32R)
        raw, _ = place("raw", [P, RING, TILE], F32)
        rstd, _ = place("rstd", [P, SEQ], F32)
        ssum, ssum_at = place("ssum", [P, SEQ], F32)
        sq, _ = place("sq", [P, 2, SEQ], F32)
        tmp, tmp_at = place("tmp", [P, 4, SEQ], F32)
        cst, _ = place("cst", [P, NCST], F32)
        ident_r, _ = place("ident_r", [P, P], F32R)
        causal_r, _ = place("causal_r", [P, P], F32R)
        vec, _ = place("vec", [P, VROWS * P], F32)
        eps, _ = place("eps", [P, 1], F32)
        fox_b, _ = place("fox_b", [P, 1], F32)
        rstd_tok, _ = place("rstd_tok", [P, TB], F32)
        neg_max, _ = place("neg_max", [P, 4, 8], F32)
        row_sum, _ = place("row_sum", [P, 4, 8], F32)
        sink_exp, _ = place("sink_exp", [P, 4, 8], F32)
        sinks, _ = place("sinks", [P, B_HEADS], F32)
        decay, _ = place("decay", [P, 2, NCH], F32)
        w_gate, _ = place("w_gate", [GLA_RANK, GLA_KW], F32)
        assert at[0] <= nc.sbuf_top, (at[0], nc.sbuf_top)

        area1, area2, area_end = hh_at + KC * SEQ * 4, hl_at + KC * SEQ * 4, (NH - KC) * SEQ * 4

        def area(start):
            state = [start]

            def take(name, shape, dt=F32):
                t, o = place(name, shape, dt, state[0])
                state[0] = o + 4 * int(np.prod(shape[1:]))
                assert state[0] <= start + area_end, (name, state[0] - start, area_end)
                return t
            return take

        a1, a2 = area(area1), area(area2)
        x_tok = a1("x_tok", [P, TB, D])
        vec_rows = a2("vec_rows", [P, VROWS, P])
        hot = a2("hot", [BUCKETS, 3 * P])
        outside = a2("outside", [B_HEADS, 3 * P])
        rel = a2("rel", [BUCKETS, B_HEADS])
        bias_rows = a2("bias_rows", [B_HEADS, 3 * P])
        a1, a2 = area(area1), area(area2)
        fqk = a1("fqk", [P, 8, SEQ])
        f_p = a1("f_p", [P, 3, BANK])
        f_pt = a1("f_pt", [P, 2, BANK])
        fv = a2("fv", [P, TB, FOX_W])
        sel = a2("sel", [P, FOX_HEADS, P], F32)
        sel_r = a2("sel_r", [P, FOX_HEADS, P], F32R)
        gate_r = a2("gate_r", [P, SEQ], F32R)
        f_o = a2("f_o", [P, 2, BANK])
        a1, a2 = area(area1), area(area2)
        gqk = a1("gqk", [P, 2, SEQ])
        gqk_raw, _ = place("gqk_raw", [P, 4, SEQ], F32, hh_at + 4 * SEQ * 4)
        k_dec = a1("k_dec", [P, 2, SEQ])
        k_end = a1("k_end", [P, 2, SEQ])
        k_tok = a1("k_tok", [P, 2, TB, P])
        state = a1("state", [P, 2, NCH, P])
        gv = a2("gv", [P, TB, GLA_HEADS * GLA_DV])
        gr = a2("gr", [P, GLA_HEADS, SEQ])
        g_a = a2("g_a", [P, 2, SEQ])
        g_cum = a2("g_cum", [P, 2, SEQ])
        g_o = a2("g_o", [P, 2, SEQ])
        gate_sig, _ = place("gate_sig", [P, GLA_HEADS, SEQ], F32, a_at)
        resets, _ = place("resets", [P, SEQ], F32, ssum_at)
        a1, a2 = area(area1), area(area2)
        xq = a1("xq", [P, KC, SEQ])
        mk = a1("mk", [P, KC, MEM])
        x_o = a1("x_o", [P, 2, BANK])
        m_hi = a2("m_hi", [P, KC, MEM], F32R)
        m_lo = a2("m_lo", [P, KC, MEM], F32R)
        mv = a2("mv", [P, 2, D])
        x_pt = a2("x_pt", [P, 2, BANK])
        mem_tok, _ = place("mem_tok", [P, 2, D], F32, area1)
        x_p, _ = place("x_p", [P, 3, BANK], F32, a_at)
        rstd_mem, _ = place("rstd_mem", [P, MEM], F32, tmp_at + 2 * SEQ * 4)
        PADW = SEQ + CONV - 1
        a1, a2 = area(area1), area(area2)
        glu = a1("glu", [P, KC, PADW])
        glu_hi = a1("glu_hi", [P, 2, -(-PADW // 8) * 8], F32R)
        glu_lo = a1("glu_lo", [P, 2, -(-PADW // 8) * 8], F32R)
        taps_hi = a1("taps_hi", [P, KC * CONV], F32R)
        taps_lo = a1("taps_lo", [P, KC * CONV], F32R)
        conv_y = a2("conv_y", [P, KC, SEQ])
        diag_hi, _ = place("diag_hi", [P, CONV, P], F32R, hh_at)
        diag_lo, _ = place("diag_lo", [P, CONV, P], F32R, hl_at)
        a1, a2 = area(area1), area(area2)
        bq = a1("bq", [P, KC, SEQ])
        bk = a1("bk", [P, 2, SEQ])
        b_p = a1("b_p", [P, 3, BANK])
        bias = a2("bias", [P, B_HEADS, 2 * P])
        bv = a2("bv", [P, TB, B_KV * B_D])
        b_pt = a2("b_pt", [P, 2, BANK])
        b_o = a2("b_o", [P, 2, BANK])
        a1 = area(area1)
        y_tok = a1("y_tok", [P, TB, D])
        y_feat, _ = place("y_feat", [P, 2, SEQ], F32, a_at)

        bias_dram = nc.dram_tensor("band_bias", (B_HEADS, P, 3 * P), F32, kind="Internal").ap()

        ps = ctx.enter_context(nc.psum_tensor("ps", [P, 8, BANK], F32))
        S_BANK = (4, 5, 6)
        PT_BANK = (7, 3)
        O_BANK = (2, 1)
        OT_BANK = 0
        BESIDE_BANK = 1

        def o_bank(kind, g):
            return O_BANK[g % 2] if kind == "x" else O_BANK[0]

        def turned(kind):
            return ps[:, OT_BANK, :] if kind == "band" else ps[:, OT_BANK, :].rearrange("p (c q) -> p c q", c=4)

        def c_(name, n=P):
            return cst[:, CST[name]:CST[name] + n]

        ident = c_("ident")

        def v_(name, i=0):
            return vec[:, VCOL[name] + i:VCOL[name] + i + 1]

        cst_in = sem("cst_in")
        consts_in = sem("consts_in")
        misc_in = sem("misc_in")
        sel_in = sem("sel_in")
        x_in = sem("x_in")
        mem_in = sem("mem_in")
        bias_out = sem("bias_out")
        bias_in = sem("bias_in")
        y_out = sem("y_out")
        raw_in = [sem(f"raw_in{i}") for i in range(RING)]
        w_hi_ready = sem("w_hi_ready")
        w_lo_ready = sem("w_lo_ready")
        tile_used = sem("tile_used")
        x_turned = sem("x_turned")
        mem_turned = sem("mem_turned")
        acc_read = sem("acc_read")
        operand_hi = sem("operand_hi")
        operand_lo = sem("operand_lo")
        square_ready = sem("square_ready")
        square_added = sem("square_added")
        stat_ready = sem("stat_ready")
        rstd_ready = sem("rstd_ready")
        head_sq = sem("head_sq")
        head_stat = sem("head_stat")
        head_rstd = sem("head_rstd")
        head_done = sem("head_done")
        consts_ready = sem("consts_ready")
        vec_turned = sem("vec_turned")
        vec_ready = sem("vec_ready")
        bias_hot = sem("bias_hot")
        bias_rows_ready = sem("bias_rows_ready")
        gate_in = sem("gate_in")
        gate_ln = sem("gate_ln")
        gate_ready = sem("gate_ready")
        scores = sem("scores")
        max_ready = sem("max_ready")
        probs = sem("probs")
        probs_turned = sem("probs_turned")
        turned_copied = sem("turned_copied")
        pv_done = sem("pv_done")
        sink_in = sem("sink_in")
        sink_ready = sem("sink_ready")
        out_scaled = sem("out_scaled")
        out_turned = sem("out_turned")
        out_hi = sem("out_hi")
        out_lo = sem("out_lo")
        g_z = sem("g_z")
        g_l = sem("g_l")
        g_cum_ready = sem("g_cum_ready")
        g_exp = sem("g_exp")
        g_dec = sem("g_dec")
        k_turned = sem("k_turned")
        k_tok_ready = sem("k_tok_ready")
        ds_ready = sem("ds_ready")
        states_ready = sem("states_ready")
        a_ready = sem("a_ready")
        a_masked = sem("a_masked")
        o_ready = sem("o_ready")
        o_copied = sem("o_copied")
        silu_ready = sem("silu_ready")
        o_done = sem("o_done")
        hidden_sig = sem("hidden_sig")
        hidden_ready = sem("hidden_ready")
        taps_ready = sem("taps_ready")
        diag_ready = sem("diag_ready")
        glu_ready = sem("glu_ready")
        glu_hi_ready = sem("glu_hi_ready")
        glu_lo_ready = sem("glu_lo_ready")
        diag_used = sem("diag_used")
        conv_summed = sem("conv_summed")
        conv_copied = sem("conv_copied")
        ln_in = sem("ln_in")
        ln_out = sem("ln_out")
        act_step = sem("act_step")
        dve_step = sem("dve_step")
        final_scaled = sem("final_scaled")
        final_turned = sem("final_turned")
        final_copied = sem("final_copied")

        def columns(w, n0, k0=0, kc=KC):
            return w.rearrange("(c p) n -> p c n", p=P)[:, k0:k0 + kc, bass.ds(n0, P)]

        def wide(w, k0, kc, n0, n):
            return w.rearrange("(c p) n -> p c n", p=P)[:, k0:k0 + kc, n0:n0 + n]

        w_in, w_out = A["w_in"], A["w_out"]
        pw1 = A["conv_w_pw1_2"][0]
        pw2 = A["conv_w_pw2_2"][0]
        w_kv = A["w_kv_2"]

        def fixed(tiles):
            return ("fixed", tiles)

        def looped(body, times, source):
            return ("looped", body, times, source)

        def down(w, parts, k_first):
            body = 4 * len(parts) if len(parts) == 3 else 4
            outs = body // len(parts)

            def source(i, j):
                m, part = j // len(parts), j % len(parts)
                k0 = k_first + sum(parts[:part])
                return columns(w, (i * outs + m) * P, k0, parts[part]), parts[part]
            return looped(body, 8 * len(parts) // body, source)

        ffn_parts = (8, 8, 6)
        SOURCES = {
            "fox_qk": looped(4, 2, lambda i, j: (columns(w_in, (4 * i + j) * P), KC)),
            "fox_v": fixed([(wide(w_in, 2 * j, 2, FV, FOX_W), 2) for j in range(4)]),
            "fox_f": fixed([(columns(w_in, FF), KC)]),
            "gla_qk": fixed([(columns(w_in, GQ + j * P), KC) for j in range(4)]),
            "gla_v": fixed([(wide(w_in, 2 * j, 2, GV, GLA_HEADS * GLA_DV), 2) for j in range(4)]),
            "gla_g": fixed([(columns(w_in, GLR), KC)]),
            "gla_r": fixed([(columns(w_in, GR + j * P), KC) for j in range(4)]),
            "mix_out": looped(4, 2, lambda i, j: (columns(w_out, (4 * i + j) * P), KC)),
            "mem_k": looped(4, 2, lambda i, j: (columns(A["xattn_wkv"], (4 * i + j) * P), KC)),
            "mem_v": fixed([(wide(A["xattn_wkv"], 2 * j, 2, D + 512 * half, 512), 2)
                            for half in range(2) for j in range(4)]),
            "x_q": looped(4, 2, lambda i, j: (columns(A["xattn_wq"], (4 * i + j) * P), KC)),
            "x_out": looped(4, 2, lambda i, j: (columns(A["xattn_wo"], (4 * i + j) * P), KC)),
            "mlp_up0": looped(4, 4, lambda i, j: (columns(A["mlp_w1"], (4 * i + j) * P), KC)),
            "mlp_down0": down(A["mlp_w2"], (8, 8), 0),
            "mlp_up1": looped(4, 4, lambda i, j: (columns(A["mlp_w1"], FF1 // 2 + (4 * i + j) * P), KC)),
            "mlp_down1": down(A["mlp_w2"], (8, 8), 16),
            "conv_in": looped(4, 4, lambda i, j: (columns(pw1, (2 * i + j // 2) * P + (j % 2) * D), KC)),
            "conv_out": looped(4, 2, lambda i, j: (columns(pw2, (4 * i + j) * P), KC)),
            "band_k": fixed([(columns(w_kv, j * P), KC) for j in range(2)]),
            "band_v": fixed([(wide(w_kv, 4 * j, 4, B_KV * B_D, B_KV * B_D), 4) for j in range(2)]),
            "band_q0": fixed([(columns(A["w_q_2"][0], j * P), KC) for j in range(2)]),
            "band_q1": fixed([(columns(A["w_q_2"][0], j * P), KC) for j in range(2, 8)]),
            "band_out": looped(4, 2, lambda i, j: (columns(A["w_o_2"][0], (4 * i + j) * P), KC)),
        }

        def ffn_up_source(layer):
            return looped(4, 11, lambda i, j: (columns(A["ffn_w_up_2"][layer],
                                                       (2 * i + j // 2) * P + (j % 2) * FF2), KC))

        for layer in range(2):
            SOURCES[f"ffn_up{layer}"] = ffn_up_source(layer)
            SOURCES[f"ffn_down{layer}"] = down(A["ffn_w_down_2"][layer], ffn_parts, 0)

        N_VEC = 4 + sum((VCOL[n] + c - 1) // P - VCOL[n] // P + 1 for n, c in VECS
                        if n and n not in ("fox_q_norm_g", "fox_k_norm_g"))
        N_MISC = 6

        block = ctx.enter_context(nc.Block())

        @block.sync
        def _(sp):
            def load_tile(t, i, per, src, kc):
                if t >= RING:
                    sp.wait_ge(w_lo_ready, t - RING + 1 + per * i)
                n = src.shape[1] * src.shape[2]
                dst = raw[:, t % RING, 0:n].rearrange("p (c n) -> p c n", c=kc)
                sp.dma_start(dst, src).then_inc(raw_in[t % RING], 16)

            def load_stage(name):
                t0 = TILE0[name]
                how = SOURCES[name]
                if how[0] == "fixed":
                    for j, (src, kc) in enumerate(how[1]):
                        load_tile(t0 + j, 0, 0, src, kc)
                    return
                _, body, times, source = how
                start = 0
                if t0 < RING:
                    for j in range(body):
                        load_tile(t0 + j, 0, 0, *source(0, j))
                    start = 1
                if times - start == 1:
                    for j in range(body):
                        load_tile(t0 + body * start + j, 0, 0, *source(start, j))
                    return
                with sp.Fori(start, times) as i:
                    for j in range(body):
                        load_tile(t0 + j, i, body, *source(i, j))

            x_rows = A["x"][0].rearrange("(b p) d -> p b d", p=P)
            sp.dma_start(cst[:], A["shape_cst"]).then_inc(cst_in, 16)
            for b in range(TB):
                sp.dma_start(x_tok[:, b, :], x_rows[:, b, :]).then_inc(x_in, 16)
            n = 0
            for name, rows in VECS:
                if name is None:
                    continue
                v = A[name]
                done = 0
                if name in ("fox_q_norm_g", "fox_k_norm_g"):
                    r = VCOL[name]
                    for half in range(2):
                        sp.dma_start(vec_rows[r:r + 1, 0, half * 64:half * 64 + 64],
                                     v.rearrange("(a d) -> a d", a=1)).then_inc(consts_in, 16)
                        n += 1
                    continue
                flat = {1: "(r p) -> r p", 2: "a (r p) -> (a r) p", 3: "a b (r p) -> (a b r) p"}[len(v.shape)]
                v = v.rearrange(flat, p=P)
                while done < rows:
                    r = VCOL[name] + done
                    m = min(rows - done, P - r % P)
                    sp.dma_start(vec_rows[r % P:r % P + m, r // P, :], v[done:done + m, :]).then_inc(consts_in, 16)
                    n += 1
                    done += m
            assert n == N_VEC, n
            load_stage("fox_qk")
            sp.wait_ge(bias_rows_ready, 1)
            sp.dma_start(bias_dram, bias_rows[:].unsqueeze(1).to_broadcast([B_HEADS, P, 3 * P]))\
              .then_inc(bias_out, 16)
            for name in ("fox_f", "fox_v", "gla_qk", "gla_v", "gla_g", "gla_r", "mix_out"):
                load_stage(name)
            sp.wait_ge(operand_lo, OP0["gla"] + 4)
            sp.dma_start(mem_tok[:], A["mem"][0].rearrange("(b p) d -> p b d", p=P)).then_inc(mem_in, 16)
            for name in ("mem_k", "mem_v", "x_q", "x_out", "mlp_up0", "mlp_down0", "mlp_up1", "mlp_down1",
                         "conv_in", "conv_out", "ffn_up0", "ffn_down0", "band_q0", "band_k", "band_v"):
                load_stage(name)
            sp.wait_ge(tile_used, TILE0["band_q0"])
            sp.dma_start(bias[:], bass.AP(bias_dram.tensor, P - 1, [[3 * P - 1, P], [3 * P * P, B_HEADS], [1, 2 * P]]))\
              .then_inc(bias_in, 16)
            for name in ("band_q1", "band_out", "ffn_up1", "ffn_down1"):
                load_stage(name)
            y_rows = out[0].rearrange("(b p) d -> p b d", p=P)
            for half in range(2):
                sp.wait_ge(final_copied, (half + 1) * KC // 2)
                cols = slice(half * D // 2, (half + 1) * D // 2)
                sp.dma_start(y_rows[:, :, cols], y_tok[:, :, cols]).then_inc(y_out, 16)
            sp.wait_ge(y_out, 16 * 2)

        @block.tensor
        def _(pe):
            mm = nc.tensor.matmul

            def wait_tile(t, more=0):
                pe.wait_ge(w_lo_ready, t + 1 + more)

            def wait_bank(o, more=0):
                if o >= 4:
                    pe.wait_ge(acc_read, o - 3 + more)

            def three(acc, l_hi, l_lo, r_hi, r_lo, start, stop):
                mm(acc, l_hi, r_hi, start=start, stop=False, skip_group_check=True)
                mm(acc, l_hi, r_lo, start=False, stop=False, skip_group_check=True)
                return mm(acc, l_lo, r_hi, start=False, stop=stop, skip_group_check=True)

            def tile_product(t, o, x_hi, x_lo, k0, kc, first, last, n=SEQ, ready=None, done=0):
                slot = t % RING
                acc = ps[:, o % 4, 0:n]
                for k in range(done, kc):
                    if ready is not None:
                        pe.wait_ge(operand_lo, ready + k + 1)
                    s = slice(k * P, (k + 1) * P)
                    ins = three(acc, w_hi[:, slot, s], w_lo[:, slot, s], x_hi[:, k0 + k, 0:n], x_lo[:, k0 + k, 0:n],
                                first and k == 0, last and k == kc - 1)
                return ins

            def outputs(name, x_hi, x_lo, ready=None, n=SEQ, after_first=None, between=None, started=None):
                t0, o0 = TILE0[name], OUT0[name]
                count = OUT_N[name]
                started = started or {}
                plain = not started and ready is None and after_first is None and between is None and count >= 8
                peel = 0 if plain else 4 if between is None and count >= 12 else count
                for j in range(peel):
                    wait_tile(t0 + j)
                    wait_bank(o0 + j)
                    tile_product(t0 + j, o0 + j, x_hi, x_lo, 0, KC, True, True, n, ready if j == 0 else None,
                                 started.get(j, 0)).then_inc(tile_used, 1)
                    if j == 0 and after_first is not None:
                        after_first()
                    if between is not None:
                        between(j)
                if peel < count:
                    with pe.Fori(peel // 4, count // 4) as i:
                        for j in range(4):
                            wait_tile(t0 + j, 4 * i)
                            wait_bank(o0 + j, 4 * i)
                            tile_product(t0 + j, o0 + j, x_hi, x_lo, 0, KC, True, True, n).then_inc(tile_used, 1)

            def down_outputs(name, parts, ready):
                t0, o0 = TILE0[name], OUT0[name]
                body = 4 * len(parts)

                def run(i):
                    for m in range(4):
                        k0 = 0
                        for q, kc in enumerate(parts):
                            t = t0 + m * len(parts) + q
                            wait_tile(t, body * i)
                            if q == 0:
                                wait_bank(o0 + m, 4 * i)
                            last = q == len(parts) - 1
                            tile_product(t, o0 + m, h_hi, h_lo, k0, kc, q == 0, last,
                                         ready=ready + k0 if m == 0 else None).then_inc(tile_used, 1)
                            k0 += kc
                with pe.Fori(0, 2) as i:
                    run(i)

            def by_token(name, x_hi, x_lo, kc, blocks, n, halves=1):
                t0, o0 = TILE0[name], OUT0[name]
                for half in range(halves):
                    tiles = KC // kc
                    for j in range(tiles):
                        t = t0 + half * tiles + j
                        wait_tile(t)
                        for b in range(blocks):
                            o = o0 + half * blocks + b
                            if j == 0:
                                wait_bank(o)
                            for k in range(kc):
                                c = j * kc + k
                                s = slice(k * n, (k + 1) * n)
                                tb = slice(b * P, (b + 1) * P)
                                w = (w_hi[:, t % RING, s], w_lo[:, t % RING, s])
                                acc = ps[:, o % 4, 0:n]
                                mm(acc, x_hi[:, c, tb], w[0], start=c == 0, stop=False, skip_group_check=True)
                                mm(acc, x_lo[:, c, tb], w[0], start=False, stop=False, skip_group_check=True)
                                ins = mm(acc, x_hi[:, c, tb], w[1], start=False, stop=c == KC - 1,
                                         skip_group_check=True)
                        ins.then_inc(tile_used, 1)

            def stat(name, bank=6, n=SEQ, tokens=0):
                pe.wait_ge(square_added, SS0[name] + KC)
                if tokens:
                    for b in range(tokens):
                        mm(ps[:, 7, b:b + 1], ssum[:, b * P:(b + 1) * P], c_("ones1024", 1), start=True, stop=True)
                mm(ps[:, bank, 0:n], c_("ones1024"), ssum[:, 0:n], start=True, stop=True).then_inc(stat_ready, 1)

            pe.wait_ge(cst_in, 16)
            pe.wait_ge(x_in, 16 * TB)
            for c in range(KC):
                wait_bank(c)
                for b in range(TB):
                    ins = nc.tensor.transpose(ps[:, c % 4, b * P:(b + 1) * P], x_tok[:, b, c * P:(c + 1) * P], ident)
                ins.then_inc(x_turned, 1)
                if c == 3:
                    pe.wait_ge(consts_in, 16 * N_VEC)
                    pe.wait_ge(misc_in, 16 * N_MISC)
                    for r, n in enumerate(VEC_ROWS):
                        ins = nc.tensor.transpose(ps[:, 4, r * P:r * P + n], vec_rows[0:n, r, :], ident[0:n, 0:n])
                    ins.then_inc(vec_turned, 1)
                    mm(ps[0:B_HEADS, 5, 0:3 * P], rel[:], hot[:], start=True, stop=True).then_inc(bias_hot, 1)

            def fox_between(j):
                if j == 1:
                    stat("x", tokens=TB)
                if j >= 1:
                    norm_stat(j - 1, "head64", [j - 1], SEQ)

            def norm_stat(s, avg, squares, n):
                pe.wait_ge(head_sq, squares[-1] + 1)
                if s >= 2:
                    pe.wait_ge(head_rstd, s - 1)
                for k, w in enumerate(squares):
                    ins = mm(ps[:, 4 + s % 2, 0:n], c_(avg), sq[:, w % 2, 0:n], start=k == 0,
                             stop=k == len(squares) - 1, skip_group_check=True)
                ins.then_inc(head_stat, 1)

            outputs("fox_qk", a_hi, a_lo, ready=OP0["x"], between=fox_between)
            norm_stat(7, "head64", [7], SEQ)
            outputs("fox_f", a_hi, a_lo)
            by_token("fox_v", a_hi, a_lo, 2, TB, FOX_W)

            def product_beside(at):
                name, j, part = at
                t = TILE0[name] + j
                if part == 0:
                    wait_tile(t)
                    pe.wait_ge(acc_read, OUT0[name] + j)
                for k in (2 * part, 2 * part + 1):
                    c = slice(k * P, (k + 1) * P)
                    ins = three(ps[:, BESIDE_BANK, :], w_hi[:, t % RING, c], w_lo[:, t % RING, c], a_hi[:, k, :],
                                a_lo[:, k, :], k == 0, k == KC - 1)
                if part == 3:
                    ins.then_inc(tile_used, 1)

            def early_out(k):
                t = TILE0["band_out"] + EARLY_OUT
                assert (OUT0["band_out"] + EARLY_OUT) % 4 == BESIDE_BANK
                if k == 0:
                    wait_tile(t)
                    pe.wait_ge(acc_read, OUT0["band_out"])
                pe.wait_ge(out_lo, ATT_G0["band"] + k + 1)
                c = slice(k * P, (k + 1) * P)
                three(ps[:, BESIDE_BANK, :], w_hi[:, t % RING, c], w_lo[:, t % RING, c], h_hi[:, k, :], h_lo[:, k, :],
                      k == 0, False)

            def attention(kind, scores_of, widths, pv_of):
                u0, units, per = ATT[kind]
                g0 = ATT_G0[kind]
                pe.wait_ge(acc_read, ATT_AFTER[kind])
                probs_at, pt_at, o_at = {"fox": (f_p, f_pt, f_o), "x": (x_p, x_pt, x_o), "band": (b_p, b_pt, b_o)}[kind]
                for s in range(units + PV_STEP[kind] + 3):
                    if s < units:
                        if u0 + s >= 3:
                            pe.wait_ge(probs, u0 + s - 2)
                        scores_of(s, S_BANK[(u0 + s) % 3]).then_inc(scores, 1)
                        if beside(kind, s):
                            product_beside(beside(kind, s))
                        if kind == "band" and s >= EARLY_UNIT:
                            early_out(s - EARLY_UNIT)
                    v = s - 2
                    if 0 <= v < units:
                        u = u0 + v
                        pe.wait_ge(probs, u + 1)
                        if u >= 2:
                            pe.wait_ge(turned_copied, u - 1)
                        for b in range(widths(v) // P):
                            ins = nc.tensor.transpose(ps[:, PT_BANK[u % 2], b * P:(b + 1) * P],
                                                      probs_at[:, u % 3, b * P:(b + 1) * P], ident)
                        ins.then_inc(probs_turned, 1)
                    v = s - PV_STEP[kind]
                    if 0 <= v < units:
                        u = u0 + v
                        g = g0 + v // per
                        pe.wait_ge(turned_copied, u + 1)
                        free = g - 1 if kind == "x" else g
                        if v % per == 0 and free >= 1:
                            pe.wait_ge(out_scaled, free)
                        pv_of(v, pt_at[:, u % 2, :], o_bank(kind, g)).then_inc(pv_done, 1)
                    v = s - PV_STEP[kind] - 2
                    if 0 <= v < units and v % per == per - 1:
                        g = g0 + v // per
                        pe.wait_ge(out_scaled, g + 1)
                        if g >= 1:
                            pe.wait_ge(out_lo, g)
                        for b in range(4):
                            ins = nc.tensor.transpose(ps[:, OT_BANK, b * P:(b + 1) * P],
                                                      o_at[:, g % 2, b * P:(b + 1) * P], ident)
                        ins.then_inc(out_turned, 1)

            def fox_scores(u, bank):
                qb, hd = u // FOX_HEADS, u % FOX_HEADS
                c, p0 = hd // 2, 64 * (hd % 2)
                n = (qb + 1) * P
                if u == 0:
                    pe.wait_ge(head_done, 8)
                    pe.wait_ge(gate_ready, 2)
                mm(ps[:, bank, 0:n], fqk[p0:p0 + 64, c, qb * P:(qb + 1) * P], fqk[p0:p0 + 64, 4 + c, 0:n],
                   start=True, stop=False, skip_group_check=True)
                mm(ps[:, bank, 0:n], sel_r[:, hd, :], gate_r[:, 0:n], start=False, stop=False, skip_group_check=True)
                return mm(ps[:, bank, n - P:n], ident_r[:], causal_r[:], start=False, stop=True, skip_group_check=True)

            def fox_pv(u, pt, bank):
                qb, hd = u // FOX_HEADS, u % FOX_HEADS
                for b in range(qb + 1):
                    ins = mm(ps[:, bank, hd * 64:hd * 64 + 64], pt[:, b * P:(b + 1) * P],
                             fv[:, b, hd * 64:hd * 64 + 64], start=b == 0, stop=b == qb, skip_group_check=True)
                return ins

            attention("fox", fox_scores, lambda u: (u // FOX_HEADS + 1) * P, fox_pv)

            pe.wait_ge(out_lo, 4)
            by_token("gla_v", a_hi, a_lo, 2, TB, GLA_HEADS * GLA_DV)
            outputs("gla_g", a_hi, a_lo)
            for p in range(2):
                pe.wait_ge(acc_read, OUT0["gla_g"] + 1)
                mm(ps[:, 4 + p, :], w_gate[:, p * P:(p + 1) * P], tmp[0:GLA_RANK, 3, :], start=True, stop=True)\
                    .then_inc(g_z, 1)
            outputs("gla_r", a_hi, a_lo)
            for p in range(2):
                pe.wait_ge(g_dec, 3 * (p + 1))
                for b in range(TB):
                    ins = nc.tensor.transpose(ps[:, 6 + p, b * P:(b + 1) * P], k_end[:, p, b * P:(b + 1) * P], ident)
                ins.then_inc(k_turned, 1)

            def gla_a(hd):
                p, p0 = hd // 2, 64 * (hd % 2)
                bank = 4 + hd % 2
                if hd >= 2:
                    pe.wait_ge(a_masked, hd - 1)
                for b in range(TB):
                    tb = slice(b * P, (b + 1) * P)
                    ins = mm(ps[:, bank, tb], k_dec[p0:p0 + 64, p, tb], gqk[p0:p0 + 64, p, tb], start=True, stop=True)
                ins.then_inc(a_ready, 1)

            def gla_stat(hd):
                pe.wait_ge(head_sq, 8 + hd + 1)
                if hd >= 1:
                    pe.wait_ge(head_rstd, 8 + hd)
                mm(ps[:, 0, :], c_("ones1024"), sq[:, hd % 2, :], start=True, stop=True).then_inc(head_stat, 1)

            gla_a(0)
            gla_a(1)
            pe.wait_ge(acc_read, OUT0["mix_out"])
            for p in range(2):
                pe.wait_ge(k_tok_ready, p + 1)
                for n in range(NCH - 1):
                    b, s0 = n // 2, 64 * (n % 2)
                    for e in range(2):
                        ins = mm(ps[64 * e:64 * e + 64, 2 * p + n % 2, b * P:(b + 1) * P],
                                 k_tok[s0:s0 + 64, p, b, 64 * e:64 * e + 64],
                                 gv[s0:s0 + 64, b, (2 * p + e) * P:(2 * p + e + 1) * P], start=True, stop=True)
                ins.then_inc(ds_ready, 1)
            for hd in range(GLA_HEADS):
                p, p0 = hd // 2, 64 * (hd % 2)
                bank = 6 + hd % 2
                pe.wait_ge(a_masked, hd + 1)
                pe.wait_ge(states_ready, p + 1)
                if hd >= 2:
                    pe.wait_ge(o_copied, hd - 1)
                for b in range(TB):
                    tb = slice(b * P, (b + 1) * P)
                    mm(ps[:, bank, tb], gv[:, b, hd * P:(hd + 1) * P], g_a[:, hd % 2, tb], start=b == 0, stop=False,
                       skip_group_check=True)
                for n in range(1, NCH):
                    ts = slice(n * CHUNK, (n + 1) * CHUNK)
                    ins = mm(ps[:, bank, ts], state[p0:p0 + 64, p, n, :], gqk[p0:p0 + 64, p, ts], start=False,
                             stop=n == NCH - 1, skip_group_check=True)
                ins.then_inc(o_ready, 1)
                if hd + 2 < GLA_HEADS:
                    gla_a(hd + 2)
                if hd >= 1:
                    gla_stat(hd - 1)
            gla_stat(GLA_HEADS - 1)

            pe.wait_ge(out_lo, 4)
            outputs("mix_out", h_hi, h_lo, ready=OP0["gla"] - 4)

            stat("x_q")
            pe.wait_ge(mem_in, 16)
            for c in range(KC):
                o = OUT0["mem_k"] - KC + c
                wait_bank(o)
                for b in range(2):
                    ins = nc.tensor.transpose(ps[:, o % 4, b * P:(b + 1) * P], mem_tok[:, b, c * P:(c + 1) * P], ident)
                ins.then_inc(mem_turned, 1)

            def mem_between(j):
                if j >= 1 and j % 2 == 0:
                    norm_stat(12 + j // 2 - 1, "ones1024", [12 + j - 2, 12 + j - 1], MEM)

            def mem_stat():
                stat("mem", bank=6, n=MEM, tokens=2)

            outputs("mem_k", m_hi, m_lo, ready=OP0["mem"], n=MEM, after_first=mem_stat, between=mem_between)
            norm_stat(15, "ones1024", [18, 19], MEM)
            by_token("mem_v", m_hi, m_lo, 2, 2, 512, halves=2)

            def xq_between(j):
                if j >= 1 and j % 2 == 0:
                    norm_stat(16 + j // 2 - 1, "ones1024", [20 + j - 2, 20 + j - 1], SEQ)

            outputs("x_q", a_hi, a_lo, ready=OP0["x_q"], between=xq_between)
            norm_stat(19, "ones1024", [26, 27], SEQ)

            def x_scores(u, bank):
                if u == 0:
                    pe.wait_ge(head_done, 20)
                for e in range(2):
                    hd = 2 * (u % 2) + e
                    qb = slice((u // 2) * P, (u // 2 + 1) * P)
                    for k in range(2):
                        ins = mm(ps[:, bank, e * MEM:(e + 1) * MEM], xq[:, 2 * hd + k, qb], mk[:, 2 * hd + k, :],
                                 start=k == 0, stop=k == 1, skip_group_check=True)
                return ins

            def x_pv(u, pt, bank):
                for e in range(2):
                    hd = 2 * (u % 2) + e
                    for b in range(2):
                        ins = mm(ps[:, bank, e * X_D:(e + 1) * X_D], pt[:, (2 * e + b) * P:(2 * e + b + 1) * P],
                                 mv[:, b, hd * X_D:(hd + 1) * X_D], start=b == 0, stop=b == 1, skip_group_check=True)
                return ins

            attention("x", x_scores, lambda u: BANK, x_pv)
            pe.wait_ge(out_lo, 12)
            outputs("x_out", h_hi, h_lo)

            outputs("mlp_up0", a_hi, a_lo, ready=OP0["mlp"], after_first=lambda: stat("mlp"))
            down_outputs("mlp_down0", (8, 8), ready=OP0["hidden0"])
            outputs("mlp_up1", a_hi, a_lo)
            down_outputs("mlp_down1", (8, 8), ready=OP0["hidden1"])

            def conv_taps(q):
                pe.wait_ge(glu_lo_ready, q + 1)
                if q >= 2:
                    pe.wait_ge(conv_copied, q - 1)
                acc = ps[:, (7, 5)[q % 2], :]
                for t in range(CONV):
                    if t % DIAG_HALF == 0:
                        pe.wait_ge(diag_ready, 4 * q + 2 * (t // DIAG_HALF) + 2)
                    ts = slice(t, t + SEQ)
                    ins = three(acc, diag_hi[:, t, :], diag_lo[:, t, :], glu_hi[:, q % 2, ts], glu_lo[:, q % 2, ts],
                                t == 0, t == CONV - 1)
                    if t == DIAG_HALF - 1:
                        ins.then_inc(diag_used, 1)
                ins.then_inc(conv_summed, 1)

            def conv_between(j):
                if j % 2 == 1 and j // 2 - 1 in PE_CONV:
                    conv_taps(PE_CONV.index(j // 2 - 1))

            outputs("conv_in", a_hi, a_lo, ready=OP0["conv"], after_first=lambda: stat("conv"), between=conv_between)
            conv_taps(len(PE_CONV) - 1)
            stat("ln_mean", bank=4)
            stat("ln_var", bank=5)
            outputs("conv_out", h_hi, h_lo, ready=OP0["conv_ln"])

            def ffn(layer):
                outputs(f"ffn_up{layer}", a_hi, a_lo, ready=OP0[f"ffn{layer}"], after_first=lambda: stat(f"ffn{layer}"))
                down_outputs(f"ffn_down{layer}", ffn_parts, ready=OP0[f"ffn_hidden{layer}"])

            ffn(0)

            outputs("band_q0", a_hi, a_lo, ready=OP0["band_q"], after_first=lambda: stat("band", tokens=TB))
            outputs("band_k", h_hi, h_lo, ready=OP0["band_kv"])
            by_token("band_v", h_hi, h_lo, 4, TB, B_KV * B_D)

            def band_scores(u, bank):
                qb, hp = u % TB, u // TB
                if qb == 0 and hp >= 2:
                    pe.wait_ge(acc_read, OUT0["band_q1"] + hp - 1)
                w = P if qb == 0 else 2 * P
                k0 = 0 if qb == 0 else (qb - 1) * P
                for e in range(2):
                    hd = 2 * hp + e
                    kv = hd // GROUP
                    p0 = 64 * (kv % 2)
                    ins = mm(ps[:, bank, e * w:(e + 1) * w], bq_at(hd, p0, qb), bk[p0:p0 + 64, kv // 2, k0:k0 + w],
                             start=True, stop=True)
                return ins

            def bq_at(hd, p0, qb):
                c, half = band_place(hd)
                assert 64 * half == p0
                return bq[p0:p0 + 64, c, qb * P:(qb + 1) * P]

            def band_pv(u, pt, bank):
                qb, hp = u % TB, u // TB
                for e in range(2):
                    hd = 2 * hp + e
                    kv = hd // GROUP
                    blocks = [0] if qb == 0 else [qb - 1, qb]
                    for k, b in enumerate(blocks):
                        s = (e * len(blocks) + k) * P
                        col = (2 * qb + e) * 64
                        ins = mm(ps[:, bank, col:col + 64], pt[:, s:s + P], bv[:, b, kv * 64:kv * 64 + 64],
                                 start=k == 0, stop=k == len(blocks) - 1, skip_group_check=True)
                return ins

            attention("band", band_scores, band_width, band_pv)
            pe.wait_ge(out_lo, 20)
            outputs("band_out", h_hi, h_lo, started={EARLY_OUT: EARLY_CHUNKS})

            ffn(1)

            stat("final")
            pe.wait_ge(acc_read, OUT0["end"])
            for c in range(KC):
                o = OUT0["end"] + c
                pe.wait_ge(final_scaled, c + 1)
                if c >= 4:
                    pe.wait_ge(final_copied, c - 3)
                for b in range(TB):
                    ins = nc.tensor.transpose(ps[:, o % 4, b * P:(b + 1) * P], y_feat[:, c % 2, b * P:(b + 1) * P], ident)
                ins.then_inc(final_turned, 1)

        @block.scalar
        def _(act):
            me = Steps(act, act_step)

            def split_hi(t, more=0):
                if t >= TILE0["end"]:
                    return
                act.wait_ge(raw_in[t % RING], 16 * (t // RING + 1) + 4 * more)
                if t >= RING:
                    act.wait_ge(tile_used, t - RING + 1 + more)
                nc.scalar.activation(w_hi[:, t % RING, :], raw[:, t % RING, :], ACT.Copy).then_inc(w_hi_ready, 1)

            def ln_exp(out_ap, in_ap, inc, scale=1.0):
                me.link(nc.scalar.activation(out_ap, in_ap, ACT.Ln, bias=eps[:], scale=scale))
                nc.scalar.activation(out_ap, out_ap, ACT.Exp, scale=-0.5).then_inc(inc, 1)

            stats = [0]

            def stat_rstd(n=SEQ, tokens=0, bank=6, to=rstd):
                stats[0] += 1
                act.wait_ge(stat_ready, stats[0])
                if tokens:
                    ln_exp(rstd_tok[:, 0:tokens], ps[:, 7, 0:tokens], rstd_ready)
                ln_exp(to[:, 0:n], ps[:, bank, 0:n], rstd_ready)

            squares, other_sums = [0], [0]

            def chunk_square(src, n=SEQ):
                k = squares[0]
                if k >= 2:
                    act.wait_ge(square_added, k - 1 + other_sums[0])
                nc.scalar.activation(sq[:, k % 2, 0:n], src, ACT.Square).then_inc(square_ready, 1)
                squares[0] += 1

            def head_square(k, src, n=SEQ):
                nc.scalar.activation(sq[:, k % 2, 0:n], src, ACT.Square).then_inc(head_sq, 1)

            def residual(name, gain, parts=1, hi=a_hi):
                t0, o0 = TILE0[name], OUT0[name]
                for m in range(8):
                    for q in range(parts):
                        split_hi(t0 + m * parts + q + AHEAD)
                    act.wait_ge(acc_read, o0 + m + 1)
                    if gain is not None:
                        nc.scalar.activation(hi[:, m, :], h[:, m, :], ACT.Copy, scale=v_(*gain(m)))\
                            .then_inc(operand_hi, 1)
                    chunk_square(h[:, m, :])

            def splits(name, lo=0, hi=None):
                n = TILE_N[name]
                for j in range(lo, n if hi is None else hi):
                    split_hi(TILE0[name] + j + AHEAD)

            def exp_and_ln():
                nc.scalar.preload_act_table_set("natural_log_exp_and_others")

            exp_and_ln()
            act.wait_ge(cst_in, 16)
            nc.scalar.activation(ident_r[:], ident, ACT.Copy).then_inc(consts_ready, 1)
            nc.scalar.activation(causal_r[:], c_("causal"), ACT.Copy).then_inc(consts_ready, 1)
            for j in range(AHEAD):
                split_hi(j)
            act.wait_ge(vec_ready, 1)
            for c in range(KC):
                act.wait_ge(acc_read, c + 1)
                nc.scalar.activation(a_hi[:, c, :], h[:, c, :], ACT.Copy, scale=v_("norm_mix_g", c))\
                    .then_inc(operand_hi, 1)
            for c in range(KC):
                chunk_square(h[:, c, :])

            def head_norms(name, k0, s0, dst, per, n=SEQ):
                t0 = TILE0[name]
                for j in range(8):
                    split_hi(t0 + j + AHEAD)
                    if j == 0 and name == "fox_qk":
                        stat_rstd(tokens=TB)
                    if j == 0 and name == "mem_k":
                        stat_rstd(n=MEM, tokens=2, to=rstd_mem)
                    act.wait_ge(acc_read, OUT0[name] + j + 1)
                    if k0 + j >= 2:
                        act.wait_ge(head_stat, s0 + (j - 2) // per + 1 if j >= 2 else s0)
                    head_square(k0 + j, dst(j), n)
                    if per == 1:
                        if j >= 1:
                            norm(s0 + j - 1, n)
                    elif j >= 3 and j % 2 == 1:
                        norm(s0 + j // 2 - 1, n)
                norm(s0 + 8 // per - 1, n)

            def norm(s, n, bank=None):
                width = GLA_DV if s < 12 else X_D
                act.wait_ge(head_stat, s + 1)
                if s >= 2:
                    act.wait_ge(head_done, s - 1)
                ln_exp(tmp[:, s % 2, 0:n], ps[:, 4 + s % 2 if bank is None else bank, 0:n], head_rstd,
                       1.0 if s < 8 else D / width)

            head_norms("fox_qk", 0, 0, lambda j: fqk[:, j, :], 1)
            act.wait_ge(sel_in, 16)
            nc.scalar.activation(sel_r[:], sel[:], ACT.Copy).then_inc(gate_ready, 1)
            splits("fox_f")
            splits("fox_v", 0, 1)
            act.wait_ge(gate_in, 1)
            rows = slice(0, FOX_HEADS)
            me.link(nc.scalar.activation(tmp[rows, 1, :], tmp[rows, 0, :], ACT.Abs))
            me.link(nc.scalar.activation(tmp[rows, 1, :], tmp[rows, 1, :], ACT.Exp, scale=-1.0))
            nc.scalar.activation(tmp[rows, 1, :], tmp[rows, 1, :], ACT.Ln, bias=1.0).then_inc(gate_ln, 1)
            splits("fox_v", 1)

            def attention(kind):
                u0, units, per = ATT[kind]
                g0 = ATT_G0[kind]
                probs_at, pt_at = {"fox": (f_p, f_pt), "x": (x_p, x_pt), "band": (b_p, b_pt)}[kind]
                for s in range(units + PV_STEP[kind] + 3):
                    at = beside(kind, s)
                    if at and at[2] == 0:
                        split_hi(TILE0[at[0]] + at[1] + AHEAD)
                    if s < units:
                        u = u0 + s
                        g = g0 + s // per
                        if kind == "fox":
                            parts = [(0, (s // 8 + 1) * P, s % 8)]
                        elif kind == "x":
                            parts = [(0, 256, 0), (256, 512, 1)]
                        else:
                            w = band_width(s) // 2
                            j = 2 * (s % 4)
                            parts = [(0, w, j), (w, 2 * w, j + 1)]
                        act.wait_ge(max_ready, u + 1)
                        if u >= 3 and kind != "band":
                            act.wait_ge(probs_turned, u - 2)
                        if s % per == 0 and g >= 4:
                            act.wait_ge(out_scaled, g - 3)
                        for a, b, j in parts:
                            src = b_p[:, u % 3, a:b] if kind == "band" else ps[:, S_BANK[u % 3], a:b]
                            ins = nc.scalar.activation(probs_at[:, u % 3, a:b], src, ACT.Exp,
                                                       bias=neg_max[:, g % 4, j:j + 1],
                                                       accum_out=row_sum[:, g % 4, j:j + 1])
                        ins.then_inc(probs, 1)
                    v = s - 2
                    if 0 <= v < units and kind == "band":
                        u = u0 + v
                        n = band_width(v)
                        act.wait_ge(probs_turned, u + 1)
                        if u >= 2:
                            act.wait_ge(pv_done, u - 1)
                        nc.scalar.activation(pt_at[:, u % 2, 0:n], ps[:, PT_BANK[u % 2], 0:n], ACT.Copy)\
                            .then_inc(turned_copied, 1)
                    v = s - PV_STEP[kind]
                    if kind == "band" and 0 <= v < units and v % per == per - 1:
                        g = g0 + v // per
                        act.wait_ge(sink_in, v // per + 1)
                        nc.scalar.activation(sink_exp[:, g % 4, :], sink_exp[:, g % 4, :], ACT.Exp)\
                            .then_inc(sink_ready, 1)
                    v = s - PV_STEP[kind] - 2
                    if 0 <= v < units and v % per == per - 1:
                        g = g0 + v // per
                        act.wait_ge(out_turned, g + 1)
                        nc.scalar.activation(group_place(kind, g - g0, h_hi), turned(kind), ACT.Copy)\
                            .then_inc(out_hi, 1)

            attention("fox")

            splits("gla_v")
            splits("gla_g")
            splits("gla_r", 0, 2)
            for p in range(2):
                act.wait_ge(g_l, 2 * p + 1)
                me.link(nc.scalar.activation(g_o[:, p, :], g_a[:, p, :], ACT.Abs))
                me.link(nc.scalar.activation(g_o[:, p, :], g_o[:, p, :], ACT.Exp, scale=-1.0))
                nc.scalar.activation(g_o[:, p, :], g_o[:, p, :], ACT.Ln, bias=1.0).then_inc(g_exp, 1)
            for p in range(2):
                act.wait_ge(g_cum_ready, 2 * p + 2)
                nc.scalar.activation(decay[:, p, :], g_cum[:, p, CHUNK - 1:SEQ:CHUNK], ACT.Exp, scale=1.0 / GLA_TAU)
                if p == 1:
                    act.wait_ge(g_dec, 3)
                nc.scalar.activation(tmp[:, 0, :], g_cum[:, p, :], ACT.Exp, scale=1.0 / GLA_TAU).then_inc(g_exp, 1)
                nc.scalar.activation(tmp[:, 1, :], g_cum[:, p, :], ACT.Exp, scale=-1.0 / GLA_TAU).then_inc(g_exp, 1)
                nc.scalar.activation(tmp[:, 2, :], g_a[:, p, :], ACT.Exp, scale=1.0 / GLA_TAU).then_inc(g_exp, 1)
            splits("gla_r", 2)
            for p in range(2):
                act.wait_ge(k_turned, p + 1)
                nc.scalar.activation(k_tok[:, p, :, :].rearrange("p b n -> p (b n)"), ps[:, 6 + p, :], ACT.Copy)\
                    .then_inc(k_tok_ready, 1)
            act.wait_ge(acc_read, OUT0["gla_r"] + GLA_HEADS)
            for hd in range(GLA_HEADS):
                nc.scalar.activation(gate_sig[:, hd, :], gr[:, hd, :], ACT.Sigmoid).then_inc(silu_ready, 1)
            exp_and_ln()
            for t in range(GLA_HEADS + 2):
                if t < GLA_HEADS:
                    act.wait_ge(o_copied, t + 1)
                    if t >= 2:
                        act.wait_ge(head_stat, 8 + t - 1)
                    head_square(8 + t, g_o[:, t % 2, :])
                if 1 <= t <= GLA_HEADS:
                    norm(8 + t - 1, SEQ, bank=0)
                if t >= 2:
                    act.wait_ge(o_done, t - 1)
                    nc.scalar.activation(h_hi[:, 4 + t - 2, :], tmp[:, 2 + t % 2, :], ACT.Copy).then_inc(operand_hi, 1)

            residual("mix_out", lambda m: ("norm_xattn_g", m))
            stat_rstd()
            for c in range(KC):
                o = OUT0["mem_k"] - KC + c
                act.wait_ge(acc_read, o + 1)
                nc.scalar.activation(m_hi[:, c, :], tmp[:, c % 2, 0:MEM], ACT.Copy, scale=v_("norm_mem_g", c))\
                    .then_inc(operand_hi, 1)
                chunk_square(tmp[:, c % 2, 0:MEM], MEM)
            head_norms("mem_k", 12, 12, lambda j: mk[:, j, :], 2, MEM)
            splits("mem_v")
            head_norms("x_q", 20, 16, lambda j: xq[:, j, :], 2)
            attention("x")
            residual("x_out", lambda m: ("norm_mlp_g", m))

            def relu_squares(name, half):
                t0 = TILE0[name]

                def body(j, i):
                    split_hi(t0 + j + AHEAD, 4 * i)
                    act.wait_ge(hidden_ready, HID0[half] + j + 1 + 4 * i)
                    nc.scalar.activation(h_hi[:, bass.ds(4 * i + j, 1), :].rearrange("p a n -> p (a n)"),
                                         tmp[:, 2 + j % 2, :], ACT.Copy).then_inc(operand_hi, 1)
                with act.Fori(0, 4) as i:
                    for j in range(4):
                        body(j, i)

            stat_rstd()
            relu_squares("mlp_up0", "hidden0")
            splits("mlp_down0")
            relu_squares("mlp_up1", "hidden1")
            residual("mlp_down1", lambda m: ("norm_mix_2", m), parts=2)

            act.wait_ge(tile_used, TILE0["conv_in"])
            nc.scalar.activation(taps_hi[:], vec[:, VCOL["conv_w_dw_2"]:NVEC], ACT.Copy).then_inc(taps_ready, 1)
            stat_rstd()
            nc.scalar.preload_act_table(ACT.Sigmoid)

            def conv_sum(q):
                m = PE_CONV[q]
                act.wait_ge(conv_summed, q + 1)
                nc.scalar.activation(conv_y[:, m, :], ps[:, (7, 5)[q % 2], :], ACT.Identity,
                                     bias=v_("conv_b_dw_2", m)).then_inc(conv_copied, 1)

            for m in range(KC):
                split_hi(TILE0["conv_in"] + 2 * m + AHEAD)
                split_hi(TILE0["conv_in"] + 2 * m + 1 + AHEAD)
                act.wait_ge(acc_read, OUT0["conv_in"] + 2 * m + 2)
                nc.scalar.activation(tmp[:, 2, :], tmp[:, 1, :], ACT.Sigmoid, bias=v_("conv_b_pw1_2", 8 + m))\
                    .then_inc(hidden_sig, 1)
                if m in PE_CONV:
                    q = PE_CONV.index(m)
                    act.wait_ge(glu_ready, q + 1)
                    if q >= 2:
                        act.wait_ge(conv_summed, q - 1)
                    nc.scalar.activation(glu_hi[:, q % 2, 0:PADW], glu[:, m, :], ACT.Copy).then_inc(glu_hi_ready, 1)
                if m - 2 in PE_CONV:
                    conv_sum(PE_CONV.index(m - 2))
            exp_and_ln()
            conv_sum(len(PE_CONV) - 1)
            other_sums[0] = KC
            for c in range(KC):
                act.wait_ge(ln_in, c + 1)
                chunk_square(conv_y[:, c, :])
            stats[0] += 1
            stat_rstd(bank=5)
            nc.scalar.preload_act_table(ACT.Sigmoid)
            for c in range(KC + 1):
                if c < KC:
                    act.wait_ge(ln_in, KC + c + 1)
                    if c >= 2:
                        act.wait_ge(ln_out, c - 1)
                    nc.scalar.activation(tmp[:, 2 + c % 2, :], conv_y[:, c, :], ACT.Sigmoid,
                                         bias=v_("conv_ln_b_2", c)).then_inc(hidden_sig, 1)
                if c >= 1:
                    act.wait_ge(ln_out, c)
                    nc.scalar.activation(h_hi[:, c - 1, :], tmp[:, (c - 1) % 2, :], ACT.Copy).then_inc(operand_hi, 1)
            exp_and_ln()
            residual("conv_out", lambda m: ("norm_ffn_2", m))

            def swiglu(layer):
                t0 = TILE0[f"ffn_up{layer}"]
                stat_rstd()
                nc.scalar.preload_act_table(ACT.Sigmoid)
                with act.Fori(0, 11) as i:
                    for m in range(2):
                        split_hi(t0 + 2 * m + AHEAD, 4 * i)
                        split_hi(t0 + 2 * m + 1 + AHEAD, 4 * i)
                        act.wait_ge(acc_read, OUT0[f"ffn_up{layer}"] + 2 * m + 1 + 4 * i)
                        nc.scalar.activation(tmp[:, 1, :], tmp[:, 0, :], ACT.Sigmoid).then_inc(hidden_sig, 1)
                        act.wait_ge(hidden_ready, HID0[f"ffn_hidden{layer}"] + m + 1 + 2 * i)
                        nc.scalar.activation(h_hi[:, bass.ds(2 * i + m, 1), :].rearrange("p a n -> p (a n)"),
                                             tmp[:, 3, :], ACT.Copy).then_inc(operand_hi, 1)
                exp_and_ln()

            swiglu(0)
            residual("ffn_down0", lambda m: ("norm_mix_2", 8 + m), parts=3)
            splits("band_q0", 0, 1)
            act.wait_ge(tile_used, TILE0["band_q0"])
            for c in range(KC):
                nc.scalar.activation(h_hi[:, c, :], h[:, c, :], ACT.Copy, scale=v_("norm_kv_2", c))\
                    .then_inc(operand_hi, 1)
            stat_rstd(tokens=TB)
            splits("band_q0", 1)
            splits("band_k")
            splits("band_v")
            attention("band")
            residual("band_out", lambda m: ("norm_ffn_2", 8 + m))
            swiglu(1)
            residual("ffn_down1", None, parts=3)
            stat_rstd()
            for c in range(KC):
                act.wait_ge(final_turned, c + 1)
                nc.scalar.activation(y_tok[:, :, c * P:(c + 1) * P],
                                     ps[:, (OUT0["end"] + c) % 4, :].rearrange("p (b n) -> p b n", b=TB), ACT.Copy)\
                    .then_inc(final_copied, 1)

        @block.gpsimd
        def _(pool):
            nc.gpsimd.dma_start(fox_b[0:FOX_HEADS, :], A["fox_b_f"].rearrange("(h o) -> h o", o=1)).then_inc(misc_in, 16)
            nc.gpsimd.dma_start(w_gate[:], A["gla_w_gate2"]).then_inc(misc_in, 16)
            nc.gpsimd.dma_start(rel[:], A["rel_bias_2"]).then_inc(misc_in, 16)
            nc.gpsimd.dma_start(sinks[:], A["sinks_2"].partition_broadcast(P)).then_inc(misc_in, 16)
            nc.gpsimd.dma_start(hot[:], A["shape_hot"]).then_inc(misc_in, 16)
            nc.gpsimd.dma_start(outside[:], A["shape_outside"]).then_inc(misc_in, 16)
            nc.gpsimd.dma_start(sel[:], A["shape_sel"].rearrange("p (h n) -> p h n", h=FOX_HEADS)).then_inc(sel_in, 16)
            for q, m in enumerate(PE_CONV):
                for half, (t0, t1) in enumerate(((0, DIAG_HALF), (DIAG_HALF, CONV))):
                    for part, (diag, w) in enumerate(((diag_hi, taps_hi), (diag_lo, taps_lo))):
                        pool.wait_ge(taps_ready, part + 1)
                        if q >= 1:
                            pool.wait_ge(diag_used if half == 0 else conv_summed, q)
                        n = t1 - t0
                        w_chunk = w[:, KC * t0 + m:KC * (t1 - 1) + m + 1:KC].bitcast(F32)
                        nc.gpsimd.tensor_tensor(diag[:, t0:t1, :], ident.unsqueeze(1).to_broadcast([P, n, P]),
                                                w_chunk.unsqueeze(2).to_broadcast([P, n, P]), ALU.mult)\
                            .then_inc(diag_ready, 1)

        @block.vector
        def _(dve):
            me = Steps(dve, dve_step)
            V = nc.vector
            f32 = lambda ap: ap.bitcast(F32)

            def split_lo(t, more=0):
                if t >= TILE0["end"]:
                    return
                dve.wait_ge(w_hi_ready, t + 1 + more)
                V.tensor_tensor(w_lo[:, t % RING, :], raw[:, t % RING, :], f32(w_hi[:, t % RING, :]), ALU.subtract)\
                    .then_inc(w_lo_ready, 1)

            def splits(name, lo=0, hi=None):
                for j in range(lo, TILE_N[name] if hi is None else hi):
                    split_lo(TILE0[name] + j + AHEAD)

            def wait_acc(name, last, more=0):
                dve.wait_ge(tile_used, TILE0[name] + last + 1 + more)

            added = [0]

            def add_square(n=SEQ, fresh=False):
                k = added[0]
                dve.wait_ge(square_ready, added_sq[0] + 1)
                src = sq[:, added_sq[0] % 2, 0:n]
                if fresh:
                    V.tensor_copy(ssum[:, 0:n], src).then_inc(square_added, 1)
                else:
                    dve.wait_ge(square_added, k)
                    V.tensor_tensor(ssum[:, 0:n], ssum[:, 0:n], src, ALU.add).then_inc(square_added, 1)
                added[0] += 1
                added_sq[0] += 1

            added_sq = [0]
            rstds = [0]

            def wait_rstd(n=1):
                rstds[0] += n
                dve.wait_ge(rstd_ready, rstds[0])

            def chunk_lo(lo, hi, src, gain, index):
                dve.wait_ge(operand_hi, index + 1)
                V.scalar_tensor_tensor(lo, src, gain, f32(hi), ALU.mult, ALU.subtract).then_inc(operand_lo, 1)

            def residual(name, op, gain, parts=1, bias_of=None):
                t0, o0 = TILE0[name], OUT0[name]
                for m in range(8):
                    for q in range(parts):
                        split_lo(t0 + m * parts + q + AHEAD)
                    wait_acc(name, m * parts + parts - 1)
                    acc = ps[:, (o0 + m) % 4, :]
                    if bias_of is None:
                        V.tensor_tensor(h[:, m, :], acc, h[:, m, :], ALU.add).then_inc(acc_read, 1)
                    else:
                        V.scalar_tensor_tensor(h[:, m, :], acc, bias_of(m), h[:, m, :], ALU.add, ALU.add)\
                            .then_inc(acc_read, 1)
                    if op is not None:
                        dve.wait_ge(acc_read, o0 + m + 1)
                        chunk_lo(a_lo[:, m, :], a_hi[:, m, :], h[:, m, :], v_(*gain(m)), OP0[op] + m)
                    add_square(fresh=m == 0)

            V.memset(eps[:], EPS).then_inc(consts_ready, 1)

            def x_chunk(c):
                dve.wait_ge(x_turned, c + 1)
                V.tensor_copy(h[:, c, :], ps[:, c % 4, :]).then_inc(acc_read, 1)

            for c in range(3):
                x_chunk(c)
            dve.wait_ge(vec_turned, 1)
            V.tensor_copy(vec[:, P:NVEC], ps[:, 4, P:NVEC])
            me.link(V.tensor_copy(vec[:, 0:VEC_ROWS[0]], ps[:, 4, 0:VEC_ROWS[0]]))
            V.tensor_scalar(v_("fox_q_norm_g"), v_("fox_q_norm_g"), FOX_D ** -0.5, None, ALU.mult)
            V.tensor_scalar(vec[:, VCOL["xattn_q_norm_g"]:VCOL["xattn_q_norm_g"] + 2],
                            vec[:, VCOL["xattn_q_norm_g"]:VCOL["xattn_q_norm_g"] + 2], X_D ** -0.5, None, ALU.mult)\
                .then_inc(vec_ready, 1)
            dve.wait_ge(vec_ready, 1)
            for j in range(AHEAD):
                split_lo(j)
            for c in range(3, KC):
                x_chunk(c)
            for c in range(KC):
                chunk_lo(a_lo[:, c, :], a_hi[:, c, :], h[:, c, :], v_("norm_mix_g", c), OP0["x"] + c)
            for c in range(KC):
                add_square(fresh=c == 0)
            dve.wait_ge(bias_hot, 1)
            V.tensor_tensor(bias_rows[:], ps[0:B_HEADS, 5, 0:3 * P], outside[:], ALU.add).then_inc(bias_rows_ready, 1)

            def head_norms(name, s0, dst, gain, per, n=SEQ, by=rstd):
                t0, o0 = TILE0[name], OUT0[name]

                def norm(s):
                    dve.wait_ge(head_rstd, s + 1)
                    for k in range(per):
                        j = (s - s0) * per + k
                        ins = V.scalar_tensor_tensor(dst(j), dst(j), gain(j), tmp[:, s % 2, 0:n], ALU.mult, ALU.mult)
                    ins.then_inc(head_done, 1)
                for j in range(8):
                    split_lo(t0 + j + AHEAD)
                    if j == 0 and name == "fox_qk":
                        wait_rstd(2)
                    if j == 0 and name == "mem_k":
                        wait_rstd(2)
                    wait_acc(name, j)
                    V.tensor_tensor(dst(j), ps[:, (o0 + j) % 4, 0:n], by[:, 0:n], ALU.mult).then_inc(acc_read, 1)
                    if per == 1:
                        if j >= 1:
                            norm(s0 + j - 1)
                    elif j >= 3 and j % 2 == 1:
                        norm(s0 + j // 2 - 1)
                norm(s0 + 8 // per - 1)

            head_norms("fox_qk", 0, lambda j: fqk[:, j, :],
                       lambda j: v_("fox_q_norm_g") if j < 4 else v_("fox_k_norm_g"), 1)
            splits("fox_f")
            splits("fox_v", 0, 1)

            def values(name, dst, n, blocks, halves=1):
                for half in range(halves):
                    for b in range(blocks):
                        o = OUT0[name] + half * blocks + b
                        wait_acc(name, TILE_N[name] // halves * (half + 1) - 1)
                        V.tensor_scalar(dst(b, half), ps[:, o % 4, 0:n], rstd_tok[:, b:b + 1], None, ALU.mult)\
                            .then_inc(acc_read, 1)

            rows = slice(0, FOX_HEADS)
            o = OUT0["fox_f"]
            wait_acc("fox_f", 0)
            dve.wait_ge(head_done, 8)
            V.tensor_tensor(tmp[rows, 0, :], ps[rows, o % 4, :], rstd[rows, :], ALU.mult).then_inc(acc_read, 1)
            dve.wait_ge(acc_read, o + 1)
            V.tensor_scalar(tmp[rows, 0, :], tmp[rows, 0, :], fox_b[rows, :], None, ALU.add).then_inc(gate_in, 1)
            me.link(V.memset(gate_r[:].bitcast(F32), 0.0))
            me.link(V.memset(tmp[rows, 3, :], 1.0))
            splits("fox_v", 1, 2)
            dve.wait_ge(gate_ln, 1)
            me.link(V.scalar_tensor_tensor(tmp[rows, 0, :], tmp[rows, 0, :], 0.0, tmp[rows, 1, :], ALU.min, ALU.subtract))
            me.link(V.tensor_tensor_scan(out=tmp[rows, 2, :], data0=tmp[rows, 3, :], data1=tmp[rows, 0, :],
                                         initial=0.0, op0=ALU.mult, op1=ALU.add))
            me.link(V.tensor_scalar(gate_r[rows, :], tmp[rows, 2, :], -1.0, None, ALU.mult))
            V.scalar_tensor_tensor(gate_r[32:32 + FOX_HEADS, :], tmp[rows, 2, :], -1.0, f32(gate_r[rows, :]),
                                   ALU.mult, ALU.subtract).then_inc(gate_ready, 1)

            splits("fox_v", 2)
            dve.wait_ge(bias_out, 16)
            values("fox_v", lambda b, half: fv[:, b, :], FOX_W, TB)
            def band_query(j, name, tile, bank):
                wait_acc(name, tile)
                for half in range(2):
                    c, dst_half = band_place(2 * j + half)
                    ins = V.scalar_tensor_tensor(bq[64 * dst_half:64 * dst_half + 64, c, :],
                                                 ps[64 * half:64 * half + 64, bank, :], B_D ** -0.5,
                                                 rstd[64 * half:64 * half + 64, :], ALU.mult, ALU.mult)
                ins.then_inc(acc_read, 1)

            def attention(kind):
                u0, units, per = ATT[kind]
                g0 = ATT_G0[kind]
                pt_at, o_at = {"fox": (f_pt, f_o), "x": (x_pt, x_o), "band": (b_pt, b_o)}[kind]
                for s in range(units + PV_STEP[kind] + 4):
                    at = beside(kind, s)
                    if at and at[2] == 0:
                        split_lo(TILE0[at[0]] + at[1] + AHEAD)
                    if s < units:
                        u = u0 + s
                        g = g0 + s // per
                        dve.wait_ge(scores, u + 1)
                        if s % per == 0 and g >= 4:
                            dve.wait_ge(out_scaled, g - 3)
                        src = ps[:, S_BANK[u % 3], :]
                        if kind == "fox":
                            V.tensor_reduce(neg_max[:, g % 4, s % 8:s % 8 + 1], src[:, 0:(s // 8 + 1) * P], axis=AX.X,
                                            op=ALU.max, negate=True).then_inc(max_ready, 1)
                        elif kind == "x":
                            V.tensor_reduce(neg_max[:, g % 4, 0:2], src.rearrange("p (a n) -> p a n", a=2), axis=AX.X,
                                            op=ALU.max, negate=True).then_inc(max_ready, 1)
                        else:
                            w = band_width(s) // 2
                            hd = 2 * (s // TB)
                            if s == 0:
                                dve.wait_ge(bias_in, 16)
                            if u >= 3:
                                dve.wait_ge(probs_turned, u - 2)
                            p3 = b_p[:, u % 3, 0:2 * w].rearrange("p (a n) -> p a n", a=2)
                            me.link(V.tensor_tensor(p3, src[:, 0:2 * w].rearrange("p (a n) -> p a n", a=2),
                                                    bias[:, hd:hd + 2, 2 * P - w:2 * P], ALU.add))
                            j = 2 * (s % 4)
                            nm = neg_max[:, g % 4, j:j + 2]
                            me.link(V.tensor_reduce(nm, p3, axis=AX.X, op=ALU.max, negate=True))
                            V.scalar_tensor_tensor(nm, sinks[:, hd:hd + 2], -1.0, nm, ALU.mult, ALU.min)\
                                .then_inc(max_ready, 1)
                    if at and at[2] == 3:
                        j = at[1]
                        if kind == "band":
                            band_query(j + 2, "band_q1", j, BESIDE_BANK)
                        else:
                            wait_acc("gla_qk", j)
                            V.tensor_tensor(gqk_raw[:, j, :], ps[:, BESIDE_BANK, :], rstd[:], ALU.mult)\
                                .then_inc(acc_read, 1)
                    v = s - 2
                    if 0 <= v < units and kind != "band":
                        u = u0 + v
                        n = (v // 8 + 1) * P if kind == "fox" else BANK
                        dve.wait_ge(probs_turned, u + 1)
                        if u >= 2:
                            dve.wait_ge(pv_done, u - 1)
                        V.tensor_copy(pt_at[:, u % 2, 0:n], ps[:, PT_BANK[u % 2], 0:n]).then_inc(turned_copied, 1)
                    v = s - PV_STEP[kind] - 3
                    if 0 <= v < units and v % per == per - 1:
                        g = g0 + v // per
                        dve.wait_ge(out_hi, g + 1)
                        V.tensor_tensor(group_place(kind, g - g0, h_lo), turned(kind),
                                        f32(group_place(kind, g - g0, h_hi)), ALU.subtract).then_inc(out_lo, 1)
                    v = s - PV_STEP[kind]
                    if 0 <= v < units and v % per == per - 1:
                        g = g0 + v // per
                        heads = 2 if kind == "x" else 8
                        rs = row_sum[:, g % 4, 0:heads]
                        dve.wait_ge(probs, u0 + v + 1)
                        if kind == "band":
                            pair = sinks[:, 2 * (g - g0):2 * (g - g0) + 2]
                            dve.wait_ge(max_ready, u0 + v + 1)
                            V.tensor_tensor(sink_exp[:, g % 4, :].rearrange("p (q e) -> p q e", e=2),
                                            pair.unsqueeze(1).to_broadcast([P, TB, 2]),
                                            neg_max[:, g % 4, :].rearrange("p (q e) -> p q e", e=2), ALU.add)\
                                .then_inc(sink_in, 1)
                            dve.wait_ge(sink_ready, v // per + 1)
                            me.link(V.tensor_tensor(rs, rs, sink_exp[:, g % 4, :], ALU.add))
                        me.link(V.reciprocal(rs, rs))
                        dve.wait_ge(pv_done, u0 + v + 1)
                        if g >= 2:
                            dve.wait_ge(out_turned, g - 1)
                        width = BANK // heads
                        V.tensor_tensor(o_at[:, g % 2, :].rearrange("p (a n) -> p a n", a=heads),
                                        ps[:, o_bank(kind, g), :].rearrange("p (a n) -> p a n", a=heads),
                                        rs.unsqueeze(2).to_broadcast([P, heads, width]), ALU.mult)\
                            .then_inc(out_scaled, 1)

            attention("fox")

            splits("gla_v")
            values("gla_v", lambda b, half: gv[:, b, :], GLA_HEADS * GLA_DV, TB)
            splits("gla_g")
            splits("gla_r", 0, 1)
            o = OUT0["gla_g"]
            wait_acc("gla_g", 0)
            V.tensor_tensor(tmp[0:GLA_RANK, 3, :], ps[0:GLA_RANK, o % 4, :], rstd[0:GLA_RANK, :], ALU.mult)\
                .then_inc(acc_read, 1)
            splits("gla_r", 1, 2)
            me.link(V.memset(resets[:], 1.0))
            me.link(V.memset(resets[:, 0:SEQ:CHUNK], 0.0))
            for p in range(2):
                dve.wait_ge(g_z, p + 1)
                V.tensor_scalar(g_a[:, p, :], ps[:, 4 + p, :], v_("gla_b_gate", p), None, ALU.add).then_inc(g_l, 1)
                dve.wait_ge(g_exp, p + 1)
                V.scalar_tensor_tensor(g_a[:, p, :], g_a[:, p, :], 0.0, g_o[:, p, :], ALU.min, ALU.subtract)\
                    .then_inc(g_l, 1)
                dve.wait_ge(g_l, 2 * p + 2)
                V.tensor_tensor_scan(out=g_cum[:, p, :], data0=resets[:], data1=g_a[:, p, :], initial=0.0,
                                     op0=ALU.mult, op1=ALU.add).then_inc(g_cum_ready, 1)
                dve.wait_ge(g_cum_ready, 2 * p + 1)
                cum = g_cum[:, p, :].rearrange("p (n c) -> p n c", c=CHUNK)
                V.tensor_tensor(g_a[:, p, :].rearrange("p (n c) -> p n c", c=CHUNK),
                                cum[:, :, CHUNK - 1:CHUNK].to_broadcast([P, NCH, CHUNK]), cum, ALU.subtract)\
                    .then_inc(g_cum_ready, 1)
            for p in range(2):
                dve.wait_ge(g_exp, 2 + 3 * p + 1)
                V.scalar_tensor_tensor(gqk[:, p, :], gqk_raw[:, p, :], GLA_DK ** -0.5, tmp[:, 0, :], ALU.mult, ALU.mult)\
                    .then_inc(g_dec, 1)
                dve.wait_ge(g_exp, 2 + 3 * p + 2)
                V.tensor_tensor(k_dec[:, p, :], gqk_raw[:, 2 + p, :], tmp[:, 1, :], ALU.mult).then_inc(g_dec, 1)
                dve.wait_ge(g_exp, 2 + 3 * p + 3)
                V.tensor_tensor(k_end[:, p, :], gqk_raw[:, 2 + p, :], tmp[:, 2, :], ALU.mult).then_inc(g_dec, 1)
            t0 = TILE0["gla_r"]
            for j in range(4):
                if j >= 2:
                    split_lo(t0 + j + AHEAD)
                o = OUT0["gla_r"] + j
                wait_acc("gla_r", j)
                V.tensor_tensor(gr[:, j, :], ps[:, o % 4, :], rstd[:], ALU.mult).then_inc(acc_read, 1)

            def mask(hd):
                dve.wait_ge(a_ready, hd + 1)
                if hd >= 2:
                    dve.wait_ge(o_ready, hd - 1)
                chunk_mask = c_("chunk").unsqueeze(1).to_broadcast([P, TB, P])
                V.tensor_tensor(g_a[:, hd % 2, :].rearrange("p (b n) -> p b n", b=TB),
                                ps[:, 4 + hd % 2, :].rearrange("p (b n) -> p b n", b=TB), chunk_mask, ALU.mult)\
                    .then_inc(a_masked, 1)

            mask(0)
            mask(1)
            for p in range(2):
                dve.wait_ge(ds_ready, p + 1)
                for n in range(1, NCH):
                    m = n - 1
                    ds = ps[:, 2 * p + m % 2, (m // 2) * P:(m // 2 + 1) * P]
                    if n == 1:
                        ins = V.tensor_copy(state[:, p, n, :], ds)
                    else:
                        ins = V.scalar_tensor_tensor(state[:, p, n, :], state[:, p, m, :], decay[:, p, m:m + 1], ds,
                                                     ALU.mult, ALU.add)
                    if n < NCH - 1:
                        me.link(ins)
                ins.then_inc(states_ready, 1)
            for hd in range(GLA_HEADS):
                dve.wait_ge(silu_ready, hd + 1)
                ins = V.tensor_tensor(gr[:, hd, :], gr[:, hd, :], gate_sig[:, hd, :], ALU.mult)
            me.link(ins)
            for t in range(GLA_HEADS + 2):
                if t < GLA_HEADS:
                    dve.wait_ge(o_ready, t + 1)
                    if t >= 2:
                        dve.wait_ge(o_done, t - 1)
                    V.tensor_copy(g_o[:, t % 2, :], ps[:, 6 + t % 2, :]).then_inc(o_copied, 1)
                    if t + 2 < GLA_HEADS:
                        mask(t + 2)
                if 1 <= t <= GLA_HEADS:
                    hd = t - 1
                    dve.wait_ge(head_rstd, 8 + hd + 1)
                    V.scalar_tensor_tensor(g_o[:, hd % 2, :], g_o[:, hd % 2, :], v_("gla_out_norm_g", hd),
                                           tmp[:, hd % 2, :], ALU.mult, ALU.mult).then_inc(head_done, 1)
                    dve.wait_ge(head_done, 8 + hd + 1)
                    if hd >= 2:
                        dve.wait_ge(operand_lo, OP0["gla"] + hd - 1)
                    V.tensor_tensor(tmp[:, 2 + hd % 2, :], g_o[:, hd % 2, :], gr[:, hd, :], ALU.mult)\
                        .then_inc(o_done, 1)
                if t >= 2:
                    hd = t - 2
                    dve.wait_ge(operand_hi, OP0["gla"] + hd + 1)
                    V.tensor_tensor(h_lo[:, 4 + hd, :], tmp[:, 2 + hd % 2, :], f32(h_hi[:, 4 + hd, :]), ALU.subtract)\
                        .then_inc(operand_lo, 1)

            residual("mix_out", "x_q", lambda m: ("norm_xattn_g", m))

            for c in range(KC):
                o = OUT0["mem_k"] - KC + c
                dve.wait_ge(mem_turned, c + 1)
                V.tensor_copy(tmp[:, c % 2, 0:MEM], ps[:, o % 4, 0:MEM]).then_inc(acc_read, 1)
                dve.wait_ge(acc_read, o + 1)
                chunk_lo(m_lo[:, c, :], m_hi[:, c, :], tmp[:, c % 2, 0:MEM], v_("norm_mem_g", c), OP0["mem"] + c)
                if c == 0:
                    dve.wait_ge(stat_ready, 2)
                add_square(n=MEM, fresh=c == 0)
            wait_rstd(1)
            head_norms("mem_k", 12, lambda j: mk[:, j, :], lambda j: v_("xattn_k_norm_g", j % 2), 2, MEM, rstd_mem)
            splits("mem_v")
            values("mem_v", lambda b, half: mv[:, b, 512 * half:512 * half + 512], 512, 2, 2)
            head_norms("x_q", 16, lambda j: xq[:, j, :], lambda j: v_("xattn_q_norm_g", j % 2), 2)
            attention("x")
            residual("x_out", "mlp", lambda m: ("norm_mlp_g", m))

            def relu_squares(name, half):
                t0, o0 = TILE0[name], OUT0[name]
                with dve.Fori(0, 4) as i:
                    for j in range(4):
                        split_lo(t0 + j + AHEAD, 4 * i)
                        wait_acc(name, j, 4 * i)
                        V.tensor_tensor(tmp[:, j % 2, :], ps[:, (o0 + j) % 4, :], rstd[:], ALU.mult)\
                            .then_inc(acc_read, 1)
                        dve.wait_ge(acc_read, o0 + j + 1 + 4 * i)
                        V.scalar_tensor_tensor(tmp[:, 2 + j % 2, :], tmp[:, j % 2, :], 0.0, tmp[:, j % 2, :], ALU.max,
                                               ALU.mult).then_inc(hidden_ready, 1)
                        dve.wait_ge(operand_hi, OP0[half] + j + 1 + 4 * i)
                        V.tensor_tensor(h_lo[:, bass.ds(4 * i + j, 1), :].rearrange("p a n -> p (a n)"),
                                        tmp[:, 2 + j % 2, :],
                                        f32(h_hi[:, bass.ds(4 * i + j, 1), :]).rearrange("p a n -> p (a n)"),
                                        ALU.subtract).then_inc(operand_lo, 1)

            wait_rstd()
            relu_squares("mlp_up0", "hidden0")
            for m in range(8):
                split_lo(TILE0["mlp_down0"] + 2 * m + AHEAD)
                split_lo(TILE0["mlp_down0"] + 2 * m + 1 + AHEAD)
                o = OUT0["mlp_down0"] + m
                wait_acc("mlp_down0", 2 * m + 1)
                V.tensor_tensor(h[:, m, :], ps[:, o % 4, :], h[:, m, :], ALU.add).then_inc(acc_read, 1)
            relu_squares("mlp_up1", "hidden1")
            residual("mlp_down1", "conv", lambda m: ("norm_mix_2", m), parts=2)

            dve.wait_ge(taps_ready, 1)
            V.tensor_tensor(taps_lo[:], vec[:, VCOL["conv_w_dw_2"]:NVEC], f32(taps_hi[:]), ALU.subtract)\
                .then_inc(taps_ready, 1)
            wait_rstd()
            me.link(V.memset(glu[:, :, 0:CONV - 1], 0.0))

            def tap(m, j):
                y = conv_y[:, m, :] if j % 2 == 0 else tmp[:, 3, :]
                w = vec[:, VCOL["conv_w_dw_2"] + 8 * j + m:VCOL["conv_w_dw_2"] + 8 * j + m + 1]
                a = glu[:, m, j:j + SEQ]
                if j >= 2:
                    dve.wait_ge(dve_step, me.done() - 1)
                if j == 0:
                    ins = V.tensor_scalar(y, a, w, v_("conv_b_dw_2", m), ALU.mult, ALU.add)
                elif j == 1:
                    ins = V.tensor_scalar(y, a, w, None, ALU.mult)
                else:
                    ins = V.scalar_tensor_tensor(y, a, w, y, ALU.mult, ALU.add)
                ins.then_inc(dve_step, 1)
                me.n += 1

            def taps(m, first, end):
                for j in range(first, end):
                    tap(m, j)
                if end == CONV:
                    dve.wait_ge(dve_step, me.done())
                    me.link(V.tensor_tensor(conv_y[:, m, :], conv_y[:, m, :], tmp[:, 3, :], ALU.add))

            def add_mean(m):
                if added[0] == SS0["ln_mean"]:
                    V.tensor_copy(ssum[:], conv_y[:, m, :]).then_inc(square_added, 1)
                else:
                    dve.wait_ge(square_added, added[0])
                    V.tensor_tensor(ssum[:], ssum[:], conv_y[:, m, :], ALU.add).then_inc(square_added, 1)
                added[0] += 1

            def glu_chunk(m):
                t0, o0 = TILE0["conv_in"] + 2 * m, OUT0["conv_in"] + 2 * m
                split_lo(t0 + AHEAD)
                wait_acc("conv_in", 2 * m)
                V.tensor_tensor(tmp[:, 0, :], ps[:, o0 % 4, :], rstd[:], ALU.mult).then_inc(acc_read, 1)
                split_lo(t0 + 1 + AHEAD)
                wait_acc("conv_in", 2 * m + 1)
                V.tensor_tensor(tmp[:, 1, :], ps[:, (o0 + 1) % 4, :], rstd[:], ALU.mult).then_inc(acc_read, 1)

            def glu_gate(m):
                dve.wait_ge(hidden_sig, m + 1)
                ins = V.scalar_tensor_tensor(glu[:, m, CONV - 1:PADW], tmp[:, 0, :], v_("conv_b_pw1_2", m),
                                             tmp[:, 2, :], ALU.add, ALU.mult)
                if m not in PE_CONV:
                    me.link(ins)
                else:
                    ins.then_inc(glu_ready, 1)

            def glu_rest(m):
                q = PE_CONV.index(m)
                dve.wait_ge(glu_hi_ready, q + 1)
                V.tensor_tensor(glu_lo[:, q % 2, 0:PADW], glu[:, m, :], f32(glu_hi[:, q % 2, 0:PADW]), ALU.subtract)\
                    .then_inc(glu_lo_ready, 1)

            half = 8
            for m in range(0, KC, 2):
                glu_chunk(m)
                glu_gate(m)
                taps(m, 0, half)
                glu_chunk(m + 1)
                glu_gate(m + 1)
                tap(m, half)
                tap(m, half + 1)
                glu_rest(m + 1)
                taps(m, half + 2, CONV)
                add_mean(m)
                if m >= 2:
                    dve.wait_ge(conv_copied, m // 2)
                    add_mean(m - 1)
            dve.wait_ge(conv_copied, len(PE_CONV))
            add_mean(KC - 1)
            dve.wait_ge(stat_ready, 6)
            for c in range(KC):
                V.tensor_tensor(conv_y[:, c, :], conv_y[:, c, :], ps[:, 4, :], ALU.subtract).then_inc(ln_in, 1)
                if c >= 1:
                    add_square(fresh=c == 1)
            add_square()
            wait_rstd()
            for c in range(KC + 2):
                if c < KC:
                    V.scalar_tensor_tensor(conv_y[:, c, :], conv_y[:, c, :], v_("conv_ln_g_2", c), rstd[:], ALU.mult,
                                           ALU.mult).then_inc(ln_in, 1)
                if 1 <= c <= KC:
                    k = c - 1
                    dve.wait_ge(hidden_sig, KC + k + 1)
                    if k >= 2:
                        dve.wait_ge(operand_lo, OP0["conv_ln"] + k - 1)
                    V.scalar_tensor_tensor(tmp[:, k % 2, :], conv_y[:, k, :], v_("conv_ln_b_2", k),
                                           tmp[:, 2 + k % 2, :], ALU.add, ALU.mult).then_inc(ln_out, 1)
                if c >= 2:
                    k = c - 2
                    dve.wait_ge(operand_hi, OP0["conv_ln"] + k + 1)
                    V.tensor_tensor(h_lo[:, k, :], tmp[:, k % 2, :], f32(h_hi[:, k, :]), ALU.subtract)\
                        .then_inc(operand_lo, 1)
            residual("conv_out", "ffn0", lambda m: ("norm_ffn_2", m), bias_of=lambda m: v_("conv_b_pw2_2", m))

            def swiglu(layer):
                name = f"ffn_up{layer}"
                t0, o0 = TILE0[name], OUT0[name]
                wait_rstd()
                with dve.Fori(0, 11) as i:
                    me.enter(i, 2)
                    for m in range(2):
                        split_lo(t0 + 2 * m + AHEAD, 4 * i)
                        wait_acc(name, 2 * m, 4 * i)
                        V.tensor_tensor(tmp[:, 0, :], ps[:, (o0 + 2 * m) % 4, :], rstd[:], ALU.mult)\
                            .then_inc(acc_read, 1)
                        split_lo(t0 + 2 * m + 1 + AHEAD, 4 * i)
                        wait_acc(name, 2 * m + 1, 4 * i)
                        V.tensor_tensor(tmp[:, 2, :], ps[:, (o0 + 2 * m + 1) % 4, :], rstd[:], ALU.mult)\
                            .then_inc(acc_read, 1)
                        dve.wait_ge(hidden_sig, KC + KC + 22 * layer + m + 1 + 2 * i)
                        me.link(V.tensor_tensor(tmp[:, 0, :], tmp[:, 0, :], tmp[:, 1, :], ALU.mult))
                        dve.wait_ge(acc_read, o0 + 2 * m + 2 + 4 * i)
                        V.tensor_tensor(tmp[:, 3, :], tmp[:, 0, :], tmp[:, 2, :], ALU.mult).then_inc(hidden_ready, 1)
                        dve.wait_ge(operand_hi, OP0[f"ffn_hidden{layer}"] + m + 1 + 2 * i)
                        V.tensor_tensor(h_lo[:, bass.ds(2 * i + m, 1), :].rearrange("p a n -> p (a n)"),
                                        tmp[:, 3, :],
                                        f32(h_hi[:, bass.ds(2 * i + m, 1), :]).rearrange("p a n -> p (a n)"),
                                        ALU.subtract).then_inc(operand_lo, 1)
                me.leave(11)

            swiglu(0)
            residual("ffn_down0", "band_q", lambda m: ("norm_mix_2", 8 + m), parts=3)
            splits("band_q0", 0, 1)
            for c in range(KC):
                chunk_lo(h_lo[:, c, :], h_hi[:, c, :], h[:, c, :], v_("norm_kv_2", c), OP0["band_kv"] + c)
            wait_rstd(2)
            splits("band_q0", 1)
            for j in range(2):
                band_query(j, "band_q0", j, (OUT0["band_q0"] + j) % 4)
            for j in range(2):
                split_lo(TILE0["band_k"] + j + AHEAD)
                o = OUT0["band_k"] + j
                wait_acc("band_k", j)
                V.tensor_tensor(bk[:, j, :], ps[:, o % 4, :], rstd[:], ALU.mult).then_inc(acc_read, 1)
            splits("band_v")
            values("band_v", lambda b, half: bv[:, b, :], B_KV * B_D, TB)
            attention("band")
            residual("band_out", "ffn1", lambda m: ("norm_ffn_2", 8 + m))
            swiglu(1)
            residual("ffn_down1", None, None, parts=3)
            wait_rstd()
            for c in range(KC):
                if c >= 2:
                    dve.wait_ge(final_turned, c - 1)
                V.scalar_tensor_tensor(y_feat[:, c % 2, :], h[:, c, :], v_("norm_final_2", c), rstd[:], ALU.mult,
                                       ALU.mult).then_inc(final_scaled, 1)


def kernel(**inputs):
    import concourse.bacc as bacc
    from concourse.bass_utils import run_bass_kernel_spmd

    nc = bacc.Bacc("TRN2", target_bir_lowering=False, num_devices=1)
    cst, sel, hot, outside = shape_constants()
    arrays = {name: np.ascontiguousarray(a) for name, a in inputs.items()}
    arrays.update(shape_cst=cst, shape_sel=sel, shape_hot=hot, shape_outside=outside)
    A = {name: nc.dram_tensor(f"in_{name}", a.shape, mybir.dt.from_np(a.dtype), kind="ExternalInput").ap()
         for name, a in arrays.items()}
    out = nc.dram_tensor("out", (1, SEQ, D), F32, kind="ExternalOutput").ap()
    build(nc, A, out)
    r = run_bass_kernel_spmd(nc, [{f"in_{name}": a for name, a in arrays.items()}], core_ids=[0])
    return r.results[0]["out"]
```
